# Optimizing a Trainium2 kernel written in Bass

```python
import jax, jax.numpy as jnp
from jax import lax
import numpy as np

D_MODEL = 1024
BATCH = 1
SEQ = 512
DEPTH = 2
DEC_BATCH = 8
DEC_SEQ = 8
PAST_LEN = 4096
PAGE_SIZE = 128

EPS = 1e-6
NEG_BIG = -1e30
D_PLE = 256
GROUP_WIDTH = D_MODEL // 4
A_HEADS = 4
A_DK = GROUP_WIDTH // A_HEADS
A_DV = GROUP_WIDTH // A_HEADS
A_WIDTH = A_HEADS * A_DV
A_CHUNK = 16
B_HEADS = 4
B_DK = GROUP_WIDTH // B_HEADS
B_DV = GROUP_WIDTH // B_HEADS
B_WIDTH = B_HEADS * B_DV
B_QKV = 2 * B_HEADS * B_DK + B_WIDTH
B_CONV = 4
B_CHUNK = 64
C_WIDTH = GROUP_WIDTH
C_CONV = 31
D_GROUPS = 4
D_WIDTH = GROUP_WIDTH
D_GC = D_WIDTH // D_GROUPS
POOL_WINDOWS = (2, 4, 8, 16)
POOL_BUF = 15
MIX_WIDTH = A_WIDTH + B_WIDTH + C_WIDTH + D_WIDTH
IN_SIZES = (A_HEADS * A_DK, A_HEADS * A_DK, A_WIDTH, A_WIDTH, B_QKV, B_WIDTH, B_HEADS, B_HEADS, 2 * C_WIDTH, D_WIDTH)
IN_COLS = 2 * A_HEADS * A_DK + 2 * A_WIDTH + B_QKV + B_WIDTH + 2 * B_HEADS + 2 * C_WIDTH + D_WIDTH
PEER_HEADS = 8
PEER_NKEYS = 128
PEER_N = PEER_NKEYS * PEER_NKEYS
PEER_DKEY = 128
PEER_HALF = PEER_DKEY // 2
PEER_TOPK = 16
PEER_BLOCK = 128

kernel_name = 'hymba_style_hgrn2_gdn_conformer_pool_peer_step'

def rmsnorm(x, g):
    xf = x.astype(jnp.float32)
    y = xf * lax.rsqrt(jnp.mean(xf * xf, axis=-1, keepdims=True) + EPS)
    return (y * g.astype(jnp.float32)).astype(x.dtype)

def layernorm(x, g, b):
    xf = x.astype(jnp.float32)
    mu = jnp.mean(xf, axis=-1, keepdims=True)
    xc = xf - mu
    var = jnp.mean(xc * xc, axis=-1, keepdims=True)
    return xc * lax.rsqrt(var + EPS) * g.astype(jnp.float32) + b.astype(jnp.float32)

def l2norm(x):
    return x * lax.rsqrt(jnp.sum(x * x, axis=-1, keepdims=True) + EPS)

def split_in(z):
    idx = np.cumsum(IN_SIZES)[:-1].tolist()
    return jnp.split(z, idx, axis=-1)

def pad_seq(t, mult):
    pad = (-t.shape[1]) % mult
    return jnp.pad(t, [(0, 0), (0, pad)] + [(0, 0)] * (t.ndim - 2))

def causal_dwconv(x, buf, w):
    xp = jnp.concatenate([buf.astype(x.dtype), x], axis=1)
    y = lax.conv_general_dilated(xp, w[:, None, :].astype(x.dtype), window_strides=(1,), padding='VALID',
                                 dimension_numbers=('NWC', 'WIO', 'NWC'), feature_group_count=x.shape[-1])
    return y, xp[:, xp.shape[1] - (w.shape[0] - 1):]

def hgrn2_chunked(q, logf, k, v, S0):
    Bn, L = q.shape[:2]
    q, logf, k, v = [pad_seq(t, A_CHUNK) for t in (q, logf, k, v)]
    N = q.shape[1] // A_CHUNK
    q, logf, k, v = [t.reshape(Bn, N, A_CHUNK, *t.shape[2:]) for t in (q, logf, k, v)]
    la = jnp.cumsum(logf, axis=2)
    causal = jnp.tril(jnp.ones((A_CHUNK, A_CHUNK), bool))
    diff = la[:, :, :, None] - la[:, :, None, :]
    dec = jnp.exp(jnp.where(causal[:, :, None, None], diff, NEG_BIG))
    scores = jnp.einsum('bnthk,bnshk,bntshk->bnhts', q, k, dec)
    o_intra = jnp.einsum('bnhts,bnshv->bnthv', scores, v)
    q_dec = q * jnp.exp(la)
    k_dec = k * jnp.exp(la[:, :, -1:] - la)
    total = jnp.exp(la[:, :, -1])

    def step(S, xs):
        qd, kd, vv, tot = xs
        o = jnp.einsum('bthk,bhkv->bthv', qd, S)
        S = tot[..., None] * S + jnp.einsum('bshk,bshv->bhkv', kd, vv)
        return S, o

    S, o_inter = lax.scan(step, S0, tuple(jnp.moveaxis(t, 1, 0) for t in (q_dec, k_dec, v, total)))
    o = o_intra + jnp.moveaxis(o_inter, 0, 1)
    o = o.reshape(Bn, N * A_CHUNK, *o.shape[3:])[:, :L]
    return o, S

def gdn_chunked(q, k, v, beta, loga, S0):
    Bn, L = q.shape[:2]
    q, k, v, beta, loga = [pad_seq(t, B_CHUNK) for t in (q, k, v, beta, loga)]
    N = q.shape[1] // B_CHUNK
    q, k, v, beta, loga = [jnp.swapaxes(t.reshape(Bn, N, B_CHUNK, *t.shape[2:]), 2, 3)
                           for t in (q, k, v, beta, loga)]
    g = jnp.cumsum(loga, axis=-1)
    ar = jnp.arange(B_CHUNK)
    causal = ar[:, None] >= ar[None, :]
    strict = ar[:, None] > ar[None, :]
    dec = jnp.exp(jnp.where(causal, g[..., :, None] - g[..., None, :], NEG_BIG))
    kk = jnp.einsum('bnhtk,bnhsk->bnhts', k, k)
    A = jnp.where(strict, beta[..., :, None] * kk * dec, 0.0)
    M = A + jnp.eye(B_CHUNK, dtype=A.dtype)
    rhs = jnp.concatenate([beta[..., None] * v, (beta * jnp.exp(g))[..., None] * k], axis=-1)
    W = lax.linalg.triangular_solve(M, rhs, left_side=True, lower=True, unit_diagonal=True)
    W1, W2 = W[..., :B_DV], W[..., B_DV:]
    qk = jnp.einsum('bnhtk,bnhsk->bnhts', q, k) * dec
    q_dec = q * jnp.exp(g)[..., None]
    k_dec = k * jnp.exp(g[..., -1:] - g)[..., None]
    total = jnp.exp(g[..., -1])

    def step(S, xs):
        w1, w2, qd, kd, qkm, tot = xs
        u = w1 - jnp.einsum('bhck,bhkv->bhcv', w2, S)
        o = jnp.einsum('bhck,bhkv->bhcv', qd, S) + jnp.einsum('bhts,bhsv->bhtv', qkm, u)
        S = tot[..., None, None] * S + jnp.einsum('bhsk,bhsv->bhkv', kd, u)
        return S, o

    S, o = lax.scan(step, S0, tuple(jnp.moveaxis(t, 1, 0) for t in (W1, W2, q_dec, k_dec, qk, total)))
    o = jnp.swapaxes(jnp.moveaxis(o, 0, 1), 2, 3)
    o = o.reshape(Bn, N * B_CHUNK, B_HEADS, B_DV)[:, :L]
    return o, S

def mixer_hgrn2(zq, zf, zi, zg, lb, norm_w, S0):
    Bn, L = zq.shape[:2]
    hd = lambda t, d: t.astype(jnp.float32).reshape(Bn, L, A_HEADS, d)
    q = jax.nn.silu(hd(zq, A_DK))
    lbh = lb.reshape(A_HEADS, A_DK)
    zff = hd(zf, A_DK)
    f = lbh + (1.0 - lbh) * jax.nn.sigmoid(zff)
    logf = jnp.log(f)
    k = (1.0 - lbh) * jax.nn.sigmoid(-zff)
    v = hd(zi, A_DV)
    o, S = hgrn2_chunked(q, logf, k, v, S0.astype(jnp.float32))
    o = rmsnorm(o, norm_w.reshape(A_HEADS, A_DV)) * jax.nn.sigmoid(hd(zg, A_DV))
    return o.reshape(Bn, L, A_WIDTH), S

def mixer_gdn(zqkv, zg, zb, za, conv_w, a_log, dt_bias, norm_w, S0, buf):
    Bn, L = zqkv.shape[:2]
    qkv, new_buf = causal_dwconv(zqkv, buf, conv_w)
    qkv = jax.nn.silu(qkv.astype(jnp.float32))
    q, k, v = jnp.split(qkv, [B_HEADS * B_DK, 2 * B_HEADS * B_DK], axis=-1)
    q = l2norm(q.reshape(Bn, L, B_HEADS, B_DK)) * (B_DK ** -0.5)
    k = l2norm(k.reshape(Bn, L, B_HEADS, B_DK))
    v = v.reshape(Bn, L, B_HEADS, B_DV)
    beta = jax.nn.sigmoid(zb.astype(jnp.float32))
    loga = -jnp.exp(a_log.astype(jnp.float32)) * jax.nn.softplus(za.astype(jnp.float32) + dt_bias.astype(jnp.float32))
    o, S = gdn_chunked(q, k, v, beta, loga, S0.astype(jnp.float32))
    o = rmsnorm(o, norm_w) * jax.nn.silu(zg.astype(jnp.float32).reshape(Bn, L, B_HEADS, B_DV))
    return o.reshape(Bn, L, B_WIDTH), S, new_buf

def mixer_conformer(zc, dw_w, dw_b, ln_g, ln_b, buf):
    a, b = jnp.split(zc, 2, axis=-1)
    u = a * jax.nn.sigmoid(b)
    y, new_buf = causal_dwconv(u, buf, dw_w)
    y = jax.nn.silu(layernorm(y + dw_b.astype(y.dtype), ln_g, ln_b))
    return y, new_buf

def mixer_pool(zd, w_pool, scale, buf, pos0):
    Bn, L, C = zd.shape
    xf = zd.astype(jnp.float32)
    xp = jnp.concatenate([buf.astype(jnp.float32), xf], axis=1)
    cs = jnp.concatenate([jnp.zeros((Bn, 1, C), jnp.float32), jnp.cumsum(xp, axis=1)], axis=1)
    end = cs[:, POOL_BUF + 1:]
    pos = pos0 + jnp.arange(L)
    means = []
    for gi, w in enumerate(POOL_WINDOWS):
        sl = slice(gi * D_GC, (gi + 1) * D_GC)
        s = end[..., sl] - cs[:, POOL_BUF + 1 - w:POOL_BUF + 1 - w + L, sl]
        cnt = jnp.minimum(w, pos + 1).astype(jnp.float32)
        means.append(s / cnt[None, :, None])
    diff = (jnp.concatenate(means, axis=-1) - xf).reshape(Bn, L, D_GROUPS, D_GC)
    y = jnp.einsum('blgc,gcd->blgd', diff, w_pool.astype(jnp.float32)).reshape(Bn, L, D_WIDTH)
    y = y * scale.astype(jnp.float32)
    return y, xp[:, xp.shape[1] - POOL_BUF:]

def peer(x, wq, keys, u_tab, v_tab):
    Bn, L, D = x.shape
    T = Bn * L
    xt = jnp.pad(x.reshape(T, D), ((0, (-T) % PEER_BLOCK), (0, 0)))
    blocks = xt.reshape(-1, PEER_BLOCK, D)

    def one(xb):
        q = (xb @ wq).astype(jnp.float32).reshape(PEER_BLOCK, PEER_HEADS, 2, PEER_HALF)
        s = jnp.einsum('thpd,hpnd->thpn', q, keys.astype(jnp.float32))
        sv, si = lax.top_k(s, PEER_TOPK)
        cand = sv[:, :, 0, :, None] + sv[:, :, 1, None, :]
        cv, ci = lax.top_k(cand.reshape(PEER_BLOCK, PEER_HEADS, PEER_TOPK * PEER_TOPK), PEER_TOPK)
        i1 = jnp.take_along_axis(si[:, :, 0], ci // PEER_TOPK, axis=-1)
        i2 = jnp.take_along_axis(si[:, :, 1], ci % PEER_TOPK, axis=-1)
        e = i1 * PEER_NKEYS + i2
        gate = jax.nn.softmax(cv, axis=-1)
        act = jax.nn.gelu(jnp.einsum('td,thkd->thk', xb, u_tab[e]).astype(jnp.float32), approximate=False)
        return jnp.einsum('thk,thkd->td', (gate * act).astype(xb.dtype), v_tab[e])

    y = lax.map(one, blocks).reshape(-1, D)[:T]
    return y.reshape(Bn, L, D).astype(x.dtype)

def run_trunk(x, p, pos0, sA, sB, cB, cC, cD, w, lb):
    h = x
    nA, nB, nbB, nbC, nbD = [], [], [], [], []
    for i in range(DEPTH):
        a = rmsnorm(h, w['norm_mix'][i])
        zaq, zaf, zai, zag, zbqkv, zbg, zbb, zba, zc, zd = split_in(a @ w['w_in'][i])
        oA, sa = mixer_hgrn2(zaq, zaf, zai, zag, lb[i], w['hgrn_norm'][i], sA[i])
        oB, sb, bb = mixer_gdn(zbqkv, zbg, zbb, zba, w['gdn_conv_w'][i], w['gdn_a_log'][i], w['gdn_dt_bias'][i],
                               w['gdn_norm'][i], sB[i], cB[i])
        oC, bc = mixer_conformer(zc, w['conf_dw_w'][i], w['conf_dw_b'][i], w['conf_ln_g'][i], w['conf_ln_b'][i], cC[i])
        oD, bd = mixer_pool(zd, w['pool_w'][i], w['pool_scale'][i], cD[i], pos0)
        mix = jnp.concatenate([oA, oB, oC, oD], axis=-1).astype(h.dtype)
        h = h + mix @ w['w_out'][i]
        h = h + peer(rmsnorm(h, w['norm_ffn'][i]), w['peer_wq'][i], w['peer_keys'][i], w['peer_u'][i], w['peer_v'][i])
        gate = jax.nn.sigmoid((rmsnorm(h, w['norm_ple'][i]) @ w['ple_gate_w'][i]).astype(jnp.float32))
        h = h + (gate * (p[i] @ w['ple_proj_w'][i]).astype(jnp.float32)).astype(h.dtype)
        nA.append(sa); nB.append(sb); nbB.append(bb); nbC.append(bc); nbD.append(bd)
    y = rmsnorm(h, w['norm_final'])
    st = lambda lst: jnp.stack(lst, axis=0).astype(x.dtype)
    return y, st(nA), st(nB), st(nbB), st(nbC), st(nbD)

def setup_inputs(seed: int = 0) -> dict:
    key = jax.random.key(seed)
    ks = jax.random.split(key, 33)
    f32 = jnp.float32
    nrm = lambda k, shape, sc: jax.random.normal(k, shape, f32) * sc
    gain = lambda k, shape: 1.0 + 0.02 * jax.random.normal(k, shape, f32)
    dt = jnp.exp(jax.random.uniform(ks[15], (DEPTH, B_HEADS), f32, float(np.log(1e-3)), float(np.log(1e-1))))
    return {
        'x_prompt': nrm(ks[0], (BATCH, SEQ, D_MODEL), 1.0),
        'x_sample': nrm(ks[1], (DEC_BATCH, DEC_SEQ, D_MODEL), 1.0),
        'state_hgrn': nrm(ks[2], (DEPTH, DEC_BATCH, A_HEADS, A_DK, A_DV), 0.5),
        'state_gdn': nrm(ks[3], (DEPTH, DEC_BATCH, B_HEADS, B_DK, B_DV), 0.3),
        'state_gdn_conv': nrm(ks[4], (DEPTH, DEC_BATCH, B_CONV - 1, B_QKV), 1.0),
        'state_conf_conv': nrm(ks[5], (DEPTH, DEC_BATCH, C_CONV - 1, C_WIDTH), 1.0),
        'state_pool': nrm(ks[6], (DEPTH, DEC_BATCH, POOL_BUF, D_WIDTH), 1.0),
        'p_prompt': nrm(ks[7], (DEPTH, BATCH, SEQ, D_PLE), 1.0),
        'p_sample': nrm(ks[8], (DEPTH, DEC_BATCH, DEC_SEQ, D_PLE), 1.0),
        'norm_mix': gain(ks[9], (DEPTH, D_MODEL)),
        'w_in': nrm(ks[10], (DEPTH, D_MODEL, IN_COLS), D_MODEL ** -0.5),
        'hgrn_lb_logits': nrm(ks[11], (DEPTH, A_HEADS * A_DK), 1.0),
        'hgrn_norm': gain(ks[12], (DEPTH, A_WIDTH)),
        'gdn_conv_w': nrm(ks[13], (DEPTH, B_CONV, B_QKV), B_CONV ** -0.5),
        'gdn_a_log': jnp.log(jax.random.uniform(ks[14], (DEPTH, B_HEADS), f32, 1.0, 16.0)),
        'gdn_dt_bias': dt + jnp.log(-jnp.expm1(-dt)),
        'gdn_norm': gain(ks[16], (DEPTH, B_DV)),
        'conf_dw_w': nrm(ks[17], (DEPTH, C_CONV, C_WIDTH), C_CONV ** -0.5),
        'conf_dw_b': nrm(ks[18], (DEPTH, C_WIDTH), 0.02),
        'conf_ln_g': gain(ks[19], (DEPTH, C_WIDTH)),
        'conf_ln_b': nrm(ks[20], (DEPTH, C_WIDTH), 0.02),
        'pool_w': nrm(ks[21], (DEPTH, D_GROUPS, D_GC, D_GC), D_GC ** -0.5),
        'pool_scale': gain(ks[22], (DEPTH, D_WIDTH)),
        'w_out': nrm(ks[23], (DEPTH, MIX_WIDTH, D_MODEL), MIX_WIDTH ** -0.5),
        'norm_ffn': gain(ks[24], (DEPTH, D_MODEL)),
        'peer_wq': nrm(ks[25], (DEPTH, D_MODEL, PEER_HEADS * PEER_DKEY), D_MODEL ** -0.5),
        'peer_keys': nrm(ks[26], (DEPTH, PEER_HEADS, 2, PEER_NKEYS, PEER_HALF), PEER_HALF ** -0.5),
        'peer_u': nrm(ks[27], (DEPTH, PEER_N, D_MODEL), D_MODEL ** -0.5),
        'peer_v': nrm(ks[28], (DEPTH, PEER_N, D_MODEL), 0.3),
        'norm_ple': gain(ks[29], (DEPTH, D_MODEL)),
        'ple_gate_w': nrm(ks[30], (DEPTH, D_MODEL, D_MODEL), D_MODEL ** -0.5),
        'ple_proj_w': nrm(ks[31], (DEPTH, D_PLE, D_MODEL), D_PLE ** -0.5),
        'norm_final': gain(ks[32], (D_MODEL,)),
    }

def reference(x_prompt, x_sample, state_hgrn, state_gdn, state_gdn_conv, state_conf_conv, state_pool,
              p_prompt, p_sample, norm_mix, w_in, hgrn_lb_logits, hgrn_norm, gdn_conv_w, gdn_a_log, gdn_dt_bias,
              gdn_norm, conf_dw_w, conf_dw_b, conf_ln_g, conf_ln_b, pool_w, pool_scale, w_out, norm_ffn,
              peer_wq, peer_keys, peer_u, peer_v, norm_ple, ple_gate_w, ple_proj_w, norm_final):
    w = dict(norm_mix=norm_mix, w_in=w_in, hgrn_norm=hgrn_norm, gdn_conv_w=gdn_conv_w, gdn_a_log=gdn_a_log,
             gdn_dt_bias=gdn_dt_bias, gdn_norm=gdn_norm, conf_dw_w=conf_dw_w, conf_dw_b=conf_dw_b,
             conf_ln_g=conf_ln_g, conf_ln_b=conf_ln_b, pool_w=pool_w, pool_scale=pool_scale, w_out=w_out,
             norm_ffn=norm_ffn, peer_wq=peer_wq, peer_keys=peer_keys, peer_u=peer_u, peer_v=peer_v,
             norm_ple=norm_ple, ple_gate_w=ple_gate_w, ple_proj_w=ple_proj_w, norm_final=norm_final)
    sm = jax.nn.softmax(hgrn_lb_logits.astype(jnp.float32), axis=0)
    lb = jnp.cumsum(sm, axis=0) - sm[0:1]
    dt = x_prompt.dtype
    zA = jnp.zeros((DEPTH, BATCH, A_HEADS, A_DK, A_DV), dt)
    zB = jnp.zeros((DEPTH, BATCH, B_HEADS, B_DK, B_DV), dt)
    zcB = jnp.zeros((DEPTH, BATCH, B_CONV - 1, B_QKV), dt)
    zcC = jnp.zeros((DEPTH, BATCH, C_CONV - 1, C_WIDTH), dt)
    zcD = jnp.zeros((DEPTH, BATCH, POOL_BUF, D_WIDTH), dt)
    y_prompt, hp, gp, gcp, ccp, pp = run_trunk(x_prompt, p_prompt, 0, zA, zB, zcB, zcC, zcD, w, lb)
    y_sample, hs, gs, gcs, ccs, ps = run_trunk(x_sample, p_sample, PAST_LEN, state_hgrn, state_gdn, state_gdn_conv,
                                               state_conf_conv, state_pool, w, lb)
    return (y_prompt, y_sample, hp, gp, gcp, ccp, pp, hs, gs, gcs, ccs, ps)


_drawn_inputs = setup_inputs


def setup_inputs(seed=0):
    import zlib

    import numpy as np

    out = dict(_drawn_inputs(seed))
    spreads = {}
    factors = {'hgrn_norm': 54.824,
     'gdn_norm': 47.753,
     'conf_ln_g': 42.589,
     'conf_ln_b': 41.225,
     'pool_scale': 34.916,
     'norm_ple': 200.0,
     'norm_final': 20.783,
     'norm_ffn': 16.716}
    for name, (base, spread) in spreads.items():
        noise = np.random.default_rng([zlib.crc32(name.encode()), seed]).standard_normal(out[name].shape)
        drawn = base * np.exp(spread * noise) if base else spread * noise
        out[name] = __import__('jax').numpy.asarray(drawn.astype(out[name].dtype))
    for name, factor in factors.items():
        out[name] = (out[name] * factor).astype(out[name].dtype)
    return out
```

```python
from contextlib import ExitStack

import numpy as np
import concourse.bass as bass
from concourse import mybir

F32 = mybir.dt.float32
F32R = mybir.dt.float32r
U32 = mybir.dt.uint32
ALU = mybir.AluOpType
ACT = mybir.ActivationFunctionType
AX = mybir.AxisListType.X

D = 1024
KT = D // 128
DEPTH = 2
SEQ = 512
NB = 8
NS = 8
SAM = NB * NS
TOK = SEQ + SAM
EPS = 1e-6
NEG = -1e30
F_MIN = 1e-18
ROWS = [128, 128, 128, 128, SAM]
COL = [0, 128, 256, 384, 512]
NT = len(ROWS)
SAMPLE = NT - 1
CH = 8
CCONV = 31
BCONV = 4
POOLB = 15
CW = SEQ + CCONV - 1
CWS = NS + CCONV - 1
QW = SEQ + BCONV - 1
QWS = NS + BCONV - 1
PW = SEQ + POOLB
PWS = NS + POOLB
HEADS = 8
NKEYS = 128
TOPK = 16
GBLK = 64
NBLK = TOK // GBLK
GROUP = 2
NGROUPS = NKEYS // GROUP
TPR = KT // GROUP
PHASE = 42816
HALF = TOK // 2
LEVELS = {False: 7, True: 3}
FM = ["ca0", "cb0", "ca1", "cb1", "p0", "p1", "k0", "k1", "k2", "k3", "k4", "k5",
      "f0", "f1", "ga0", "ga1", "q0", "q1", "gb0", "gb1"]
NFM = len(FM)
TMW = 256 + 8
NWF = 3


def constants():
    t = np.arange(128)
    s = t[:, None]
    lower = lambda size: (s // size == t // size)
    put = {}
    put["ident"] = np.eye(128)
    put["ones"] = np.ones((128, 128))
    put["tri_p"] = s <= t
    put["tri_s"] = (lower(NS) & (s <= t))[:, :SAM]
    put["below_p"] = np.where(s > t, 0, NEG)
    put["below_s"] = np.where(lower(NS) & (s > t), 0, NEG)[:, :SAM]
    put["upto_p"] = np.where(s <= t, 0, NEG)
    put["upto_s"] = np.where(lower(NS) & (s <= t), 0, NEG)[:, :SAM]
    put["levels"] = np.concatenate(
        [lower(2 << l) & ((s >> l) % 2 == 1) & ((t >> l) % 2 == 0) for l in range(7)], 1)
    put["chunk_p"] = lower(16) & (s <= t)
    put["chunk_s"] = (lower(8) & (s <= t))[:, :SAM]
    put["same_s"] = lower(NS)[:, :SAM]
    put["member_p"] = s // 16 == t[None, :CH]
    put["member_s"] = s // 8 == t[None, :CH]
    put["pair"] = s // 64 == t[None, :2]
    put["halves"] = s // 64 == t // 64
    tok = np.arange(TOK)
    put["carry"] = np.broadcast_to(np.where(tok < SEQ, tok % 16 != 0, tok % NS != 0), (128, TOK))
    put["iota"] = np.broadcast_to(t, (128, 128))
    windows = np.stack([np.where(t < 64, 2, 4), np.where(t < 64, 8, 16)], 1)
    put["inv_count"] = (1.0 / np.minimum(windows[:, :, None], np.arange(16) + 1)).reshape(128, 32)
    put["inv_window"] = 1.0 / windows
    put["eps"] = np.full((128, 1), EPS)
    at, parts, n = {}, [], 0
    for name, a in put.items():
        a = np.asarray(a, np.float32)
        at[name] = (n, a.shape[1])
        parts.append(a)
        n += a.shape[1]
    return at, np.ascontiguousarray(np.concatenate(parts, 1))


PARAMS = [("gain", 24), ("hnorm", 2), ("gnorm", 1), ("qconv", 24), ("cconv", 62), ("cbias", 2), ("cgain", 2),
          ("cshift", 2), ("pscale", 2), ("poolw", 128), ("alog", 4), ("dt", 4), ("logits", 4)]
PARW = sum(w for _, w in PARAMS)


class Counts:

    def __init__(self, known):
        self.known, self.now, self.marks = known, {}, {}

    def up(self, name, by, label):
        self.now[name] = self.now.get(name, 0) + by
        if label:
            assert label not in self.marks, label
            self.marks[label] = (name, self.now[name])

    def same(self, label, as_label):
        self.marks[label] = self.marks[as_label]


class Engine:

    def __init__(self, eng, name, counts):
        self.eng, self.name, self.counts, self.waited = eng, name, counts, {}

    def wait_ge(self, sem, value):
        if value > self.waited.get(id(sem), 0):
            self.waited[id(sem)] = value
            self.eng.wait_ge(sem, value)

    def did(self, ins, *label):
        self.counts.up(self.name, 1, label)

    def sent(self, name, ins, *label):
        self.counts.up(name, 16, label)


def trunk(nc, din, dout, gates_dram, known):
    ctx = ExitStack()
    counts = Counts(known and known["marks"])
    sems = {}

    def sem(name):
        if name not in sems:
            sems[name] = ctx.enter_context(nc.semaphore(name))
        return sems[name]

    def at(*label):
        return 1 if known is None else known["marks"][label][1]

    def made(*label):
        return (sem("pe_done"), 1) if known is None else (sem(known["marks"][label][0]), at(*label))

    def count(name):
        return counts.now.get(name, 0)
    CAT, _ = constants()
    CONSTW = sum(w for _, w in CAT.values())

    place = {}

    def memory(scope, name, size, kind=F32):
        place.update(tensor=scope.enter_context(nc.sbuf_tensor(name, [128, size], kind)), at=0, size=size)

    PS = ctx.enter_context(nc.psum_tensor("banks", [128, 8, 512], F32))

    def region(*shape):
        n = int(np.prod(shape))
        a = place["tensor"][:, place["at"]:place["at"] + n]
        place["at"] += n
        assert place["at"] <= place["size"], (place["at"], place["size"])
        if len(shape) == 2:
            return a.rearrange("p (a b) -> p a b", a=shape[0])
        if len(shape) == 3:
            return a.rearrange("p (a b c) -> p a b c", a=shape[0], b=shape[1])
        if len(shape) == 4:
            return a.rearrange("p (a b c d) -> p a b c d", a=shape[0], b=shape[1], c=shape[2])
        return a

    memory(ctx, "kept", NT * D + CONSTW + PARW + 16 + 2 * D + 12)
    H = region(NT, D)
    CONST = region(CONSTW)
    PAR = region(PARW)
    SS = region(16)
    XN = region(2, D)
    LBV = region(12)
    memory(ctx, "x", KT * TOK)
    XT = region(KT, TOK)
    place["at"] = 0
    XC = region(6, TOK)
    GS = region(2, NB, 64)
    place["at"] = 0
    OH1 = region(2, 8, 128)
    OH2 = region(2, 8, 128)
    STG = region(3, GBLK)
    place["at"] = 0
    ACC = region(KT, TOK)
    phase = ExitStack()
    memory(phase, "mixers", PHASE - KT * TOK)
    MIXT = region(KT, TOK)
    Wbase = place["at"]
    WF = region(NWF, D)
    WT = region(KT, TMW)
    place["at"] = Wbase
    WO = region(KT, D)
    ZQ = region(2, TOK)
    LF = region(2, TOK)
    KF = region(2, TOK)
    LA = region(2, TOK)
    EL = region(2, TOK)
    KD = region(2, TOK)
    GA = region(2, TOK)
    GB = region(2, TOK)
    QR = region(6, QW + NB * QWS)
    VT = region(NT, 256)
    BA = region(NT, 8)
    TMP = place["at"]
    CU = region(2, CW + NB * CWS)
    CS = region(2, TOK)
    CY = region(2, TOK)
    CQ = region(2, TOK)
    PX = region(2, PW + NB * PWS)
    PA = region(2, PW + NB * PWS)
    PB = region(2, PW + NB * PWS)
    place["at"] = TMP
    PROD = region(2048)
    HQK = region(2048)
    ST = region(4, 128)
    VM = region(4, CH, 64)
    HS = region(2, CH + 1, 64)
    KDT = region(256)
    HSQ = region(2, 128)
    HRT = region(2, 128)
    HON = region(2, 128)
    place["at"] = TMP
    QKN = region(8, 64)
    QDN = region(4, 64)
    RH1 = region(4, 64)
    RH2 = region(4, 64)
    KDEC = region(4, 64)
    QKT = region(6, 128)
    DA = region(4, 128)
    DQ = region(4, 128)
    XI = region(4, 128)
    TI = region(4, 128)
    PI = region(4, 128)
    AM = region(2, 4, 128)
    W2T = region(2, 128)
    UT = region(2, 128)
    UU = region(4, 64)
    UM = region(4, NB, 64)
    LB = region(4, 128)
    GSQ = region(2, 128)
    GRT = region(2, 128)
    GON = region(2, 128)
    GSM = region(160)
    place["at"] = 0
    WG = region(KT, D)
    WP = region(2, D)
    PT = region(2, TOK)
    SG = region(2, D)
    TP = region(2, D)
    GF = region(D)
    phase.close()
    phase = ExitStack()
    memory(phase, "peer_places", 3 * TOK)
    IT = region(3, TOK)
    memory(phase, "peer_x_parts", 2 * KT * TOK, F32R)
    XR = region(2, KT, TOK)
    part = ExitStack()
    memory(part, "peer_scores", PHASE - (3 * KT + 3) * TOK)
    WQ = region(NWF, D)
    QT = region(HEADS, TOK)
    KEYS = region(HEADS, NKEYS)
    SCO = region(2, 2048)
    SV = region(256)
    SI = region(256).bitcast(U32)
    SIF = region(256)
    CAND = region(2048)
    CV = region(128)
    CI = region(128).bitcast(U32)
    CI2 = region(2, 128).bitcast(U32)
    CIF = region(2, 128)
    PICK = region(2048)
    IGT = region(3, 128)
    GSUM = region(16)
    place["at"] = 0
    GBUF = region(3, NKEYS, GBLK)
    part.close()
    memory(phase, "experts_parts", 4 * D + 4 * GROUP * (TOK + D), F32R)
    UR = region(2, 2, D)
    HR = region(2 * GROUP, 2, TOK)
    VR = region(2 * GROUP, 2, D)
    memory(phase, "experts", 3 * GROUP * D + 2 * TOK + 2 * GROUP * TOK)
    US = region(2 * GROUP, D)
    VS = region(GROUP, D)
    GE = region(2, TOK)
    GT = region(2, NBLK, GROUP * GBLK)
    phase.close()

    def const(name):
        o, w = CAT[name]
        return CONST[:, o:o + w]

    par_at, n = {}, 0
    for name, w in PARAMS:
        par_at[name] = (n, w)
        n += w

    def par(name):
        o, w = par_at[name]
        return PAR[:, o:o + w]

    ident, ones = const("ident"), const("ones")

    fills = {"n": 0, "start": 0, "order": []}

    def bank_free():
        n = fills["n"]
        if n - 8 < fills["start"]:
            return pe_done, 0
        return made("drained", *fills["order"][n - 8])

    def fill(*label):
        fills["order"].append(label)
        fills["n"] += 1
        return PS[:, (fills["n"] - 1) % 8, :]

    def bank(*label):
        return PS[:, 0 if known is None else known["banks"][label], :]

    pe_done, act_done, dve_done, pool_done = sem("pe_done"), sem("act_done"), sem("dve_done"), sem("pool_done")
    d_gload = [sem(f"gates_loaded{i}") for i in range(2)]
    d_gstore = [sem(f"gates_stored{i}") for i in range(3)]
    d_ut = [sem(f"u_loaded{i}") for i in range(2 * GROUP)]
    d_v = [sem(f"v_loaded{i}") for i in range(2)]
    staged, oh1_ready, oh2_ready = sem("staged"), sem("oh1_ready"), sem("oh2_ready")
    scattered, gates_copied = sem("scattered"), sem("gates_copied")
    u_done, gelu_done, hm_done = sem("u_done"), sem("gelu_done"), sem("hm_done")
    v_done, acc_done = sem("v_done"), sem("acc_done")
    u_rounded, u_split, v_rounded, v_split = sem("u_rounded"), sem("u_split"), sem("v_rounded"), sem("v_split")
    gated, gated_rounded = sem("gated"), sem("gated_rounded")

    def halo(t, c, width, halo_w, step, shift=0, n=SEQ):
        return t[:, c, halo_w + shift:halo_w + shift + n]

    def halo_s(t, c, width, halo_w, step, shift=0, n=NS):
        return t[:, c, width:].rearrange("p (b w) -> p b w", b=NB)[:, :, halo_w + shift:halo_w + shift + n]

    def sam(t, c):
        return t[:, c, SEQ:TOK].rearrange("p (b w) -> p b w", b=NB)

    def bank_s(b):
        return b[:, 0:SAM].rearrange("p (b w) -> p b w", b=NB)

    def bc(ap, axis, n):
        u = ap.unsqueeze(axis)
        shape = list(u.shape)
        shape[axis] = n
        return u.broadcast_to(shape)

    block = ctx.enter_context(nc.Block())

    @block.sync
    def _(eng):
        sp = Engine(eng, "sp_done", counts)

        for j in range(3):
            eng.sem_inc(d_gstore[j], 16)
        sp.sent("const_loaded", eng.dma_start(CONST, din["consts"]).then_inc(sem("const_loaded"), 16), "consts")
        for i in range(NT - 1):
            sp.sent(f"h{i}_loaded", eng.dma_start(H[:, i, :], din["x_prompt"][COL[i]:COL[i] + 128, :]).then_inc(sem(f"h{i}_loaded"), 16), "x", i)
        sp.sent("h4_loaded", eng.dma_start(H[0:SAM, SAMPLE, :], din["x_sample"]).then_inc(sem("h4_loaded"), 16), "x", SAMPLE)
        for L in range(DEPTH):
            if L > 0:
                sp.wait_ge(dve_done, at("ple_done", L - 1))
            sp.sent("params_loaded", eng.dma_start(PAR, din["params"][L]).then_inc(sem("params_loaded"), 16), "params", L)
            for j in range(NFM):
                if j >= NWF:
                    sp.wait_ge(pe_done, at("fm", L, j - NWF))
                sp.sent(f"wf{j % NWF}_loaded", eng.dma_start(WF[:, j % NWF, :], din["w_fm"][L, j]).then_inc(sem(f"wf{j % NWF}_loaded"), 16), "wf", L, j)
                if j == 1:
                    sp.sent("wt_loaded", eng.dma_start(WT, din["w_tm"][L]).then_inc(sem("wt_loaded"), 16), "wt", L)
            for c in range(2):
                sp.sent(f"cu{c}_loaded", eng.dma_start(CU[:, c, CW:].rearrange("p (b w) -> p b w", b=NB)[:, :, 0:CCONV - 1], din["s_conf"][L, :, c]).then_inc(sem(f"cu{c}_loaded"), 16), "cu", L, c)
                sp.sent(f"px{c}_loaded", eng.dma_start(PX[:, c, PW:].rearrange("p (b w) -> p b w", b=NB)[:, :, 0:POOLB], din["s_pool"][L, :, c]).then_inc(sem(f"px{c}_loaded"), 16), "px", L, c)
            for c in range(6):
                sp.sent(f"qr{c}_loaded", eng.dma_start(QR[:, c, QW:].rearrange("p (b w) -> p b w", b=NB)[:, :, 0:BCONV - 1], din["s_qkv"][L, :, c]).then_inc(sem(f"qr{c}_loaded"), 16), "qr", L, c)
            for c in range(2):
                sp.wait_ge(dve_done, at("cu_ready", L, c))
                sp.wait_ge(sem(f"cu{c}_loaded"), at("cu", L, c))
                sp.sent("conf_stored", eng.dma_start(dout["conf_p"][L, :, c], CU[:, c, SEQ:CW]).then_inc(sem("conf_stored"), 16))
                sp.sent("conf_stored", eng.dma_start(dout["conf_s"][L, :, c], CU[:, c, CW:].rearrange("p (b w) -> p b w", b=NB)[:, :, NS:CWS]).then_inc(sem("conf_stored"), 16), "conf_out", L, c)
            for c in range(2):
                sp.wait_ge(dve_done, at("px_ready", L, c))
                sp.wait_ge(sem(f"px{c}_loaded"), at("px", L, c))
                sp.sent("pool_stored", eng.dma_start(dout["pool_p"][L, :, c], PX[:, c, SEQ:PW]).then_inc(sem("pool_stored"), 16))
                sp.sent("pool_stored", eng.dma_start(dout["pool_s"][L, :, c], PX[:, c, PW:].rearrange("p (b w) -> p b w", b=NB)[:, :, NS:PWS]).then_inc(sem("pool_stored"), 16), "pool_out", L, c)
            for c in range(6):
                sp.wait_ge(dve_done, at("qr_ready", L, c))
                sp.wait_ge(sem(f"qr{c}_loaded"), at("qr", L, c))
                sp.sent("qkv_stored", eng.dma_start(dout["qkv_p"][L, :, c], QR[:, c, SEQ:QW]).then_inc(sem("qkv_stored"), 16))
                sp.sent("qkv_stored", eng.dma_start(dout["qkv_s"][L, :, c], QR[:, c, QW:].rearrange("p (b w) -> p b w", b=NB)[:, :, NS:QWS]).then_inc(sem("qkv_stored"), 16), "qkv_out", L, c)
            sp.wait_ge(pe_done, at("w_in", L))
            for k in range(0, KT, 2):
                sp.sent(f"wo{k}_loaded", eng.dma_start(WO[:, k:k + 2, :], din["w_out"][L, :, k:k + 2]).then_inc(sem(f"wo{k}_loaded"), 16), "wo", L, k)
            sp.wait_ge(dve_done, at("hs_prompt", L))
            sp.sent("hs_p_stored", eng.dma_start(dout["hgrn_p"][L], HS[:, :, 0, :]).then_inc(sem("hs_p_stored"), 16), "hs_out", L)
            sp.wait_ge(sem("hs_p_stored"), at("hs_out", L))
            sp.sent("hs_loaded", eng.dma_start(HS[:, :, 0:NB, :], din["s_hgrn"][L]).then_inc(sem("hs_loaded"), 16), "hs", L)
            sp.wait_ge(dve_done, at("hs_sample", L))
            sp.sent("hs_s_stored", eng.dma_start(dout["hgrn_s"][L], HS[:, :, 0:NB, :]).then_inc(sem("hs_s_stored"), 16), "hs2_out", L)
            sp.wait_ge(dve_done, at("gs_prompt", L))
            sp.sent("gs_p_stored", eng.dma_start(dout["gdn_p"][L], GS[:, :, 0, :]).then_inc(sem("gs_p_stored"), 16), "gs_out", L)
            sp.wait_ge(sem("gs_p_stored"), at("gs_out", L))
            sp.sent("gs_loaded", eng.dma_start(GS[:, :, :, :], din["s_gdn"][L]).then_inc(sem("gs_loaded"), 16), "gs", L)
            sp.wait_ge(dve_done, at("gs_sample", L))
            sp.sent("gs_s_stored", eng.dma_start(dout["gdn_s"][L], GS[:, :, :, :]).then_inc(sem("gs_s_stored"), 16), "gs2_out", L)
            sp.wait_ge(dve_done, at("h", 3 * L + 1, NT - 1))
            for j in range(KT):
                if j >= NWF:
                    sp.wait_ge(pe_done, at("wq", L, j - NWF))
                sp.sent(f"wf{j % NWF}_loaded", eng.dma_start(WQ[:, j % NWF, :], din["peer_wq"][L, j]).then_inc(sem(f"wf{j % NWF}_loaded"), 16), "wqload", L, j)
                if j == 0:
                    sp.sent("keys_loaded", eng.dma_start(KEYS, din["peer_keys"][L]).then_inc(sem("keys_loaded"), 16), "keys", L)
            with eng.Fori(0, NBLK // 3) as it:
                for j in range(3):
                    blk = it * 3 + j
                    eng.wait_ge(gates_copied, (blk + NBLK * L) * 16 + 16 + 4)
                    eng.dma_start(gates_dram[bass.ds(blk, 1)].rearrange("a p i t -> (a p) i t"),
                                  GBUF[:, j]).then_inc(d_gstore[j], 16)
            for j in range(3):
                eng.wait_ge(d_gstore[j], 16 * (NBLK // 3 * (L + 1) + 1))
            sp.wait_ge(dve_done, at("hm_free", L))
            with eng.Fori(0, NGROUPS // 2) as it:
                for par_ in range(2):
                    g = it * 2 + par_
                    for i in range(GROUP):
                        row = (g + NGROUPS * L) * GROUP + i
                        slot = par_ * GROUP + i
                        eng.wait_ge(u_split, row + 1)
                        eng.dma_start(US[:, slot, :],
                                      din["peer_ut"][L, bass.ds(g * GROUP + i, 1)].rearrange("a p d -> (a p) d"))\
                            .then_inc(d_ut[slot], 16)
                        if i == 0:
                            eng.wait_ge(hm_done, row + GROUP)
                            eng.dma_start(GT[:, par_], gates_dram[:, :, bass.ds(g * GROUP, GROUP), :]
                                          .rearrange("b p i t -> p b (i t)")).then_inc(d_gload[par_], 16)
                        eng.wait_ge(v_split, row + 1)
                        eng.dma_start(VS[:, i, :],
                                      din["peer_v"][L, bass.ds(g * GROUP + i, 1)].rearrange("a p d -> (a p) d"))\
                            .then_inc(d_v[i], 16)
            sp.wait_ge(dve_done, at("h", 3 * L + 2, NT - 1))
            for k in range(0, KT, 4):
                sp.sent(f"wg{k}_loaded", eng.dma_start(WG[:, k:k + 4, :], din["ple_gate"][L, :, k:k + 4]).then_inc(sem(f"wg{k}_loaded"), 16), "wg", L, k)
            sp.sent("wp_loaded", eng.dma_start(WP, din["ple_proj"][L]).then_inc(sem("wp_loaded"), 16), "wp", L)
            sp.sent("pt_loaded", eng.dma_start(PT, din["p_t"][L]).then_inc(sem("pt_loaded"), 16), "pt", L)
            if L == DEPTH - 1:
                sp.sent("gf_loaded", eng.dma_start(GF, din["norm_final"]).then_inc(sem("gf_loaded"), 16), "gf")
        for i in range(NT):
            sp.wait_ge(dve_done, at("y", i))
            dst = dout["y_prompt"][COL[i]:COL[i] + 128, :] if i < SAMPLE else dout["y_sample"]
            sp.sent(f"y{i % 2}_stored", eng.dma_start(dst, XN[0:ROWS[i], i % 2, :]).then_inc(sem(f"y{i % 2}_stored"), 16), "y_out", i)
        for name in ("conf", "pool", "qkv", "hs_p", "hs_s", "gs_p", "gs_s", "y0", "y1"):
            eng.wait_ge(sem(name + "_stored"), count(name + "_stored"))

    @block.tensor
    def _(eng):
        pe = Engine(eng, "pe_done", counts)
        mm = eng.matmul
        eng.sem_inc(u_done, 2)
        eng.sem_inc(v_done, 2 * KT)
        eng.sem_inc(scattered, 4)


        def row_tiles_change(ins):
            pe.did(ins.then_inc(pe_done, 1))
            pe.wait_ge(pe_done, count("pe_done"))

        def norm_turn(u):
            for i in range(NT):
                R = ROWS[i]
                pe.wait_ge(dve_done, at("xn", u, i))
                if u == 0 and i == 0:
                    pe.wait_ge(sem("const_loaded"), at("consts"))
                for half in range(2):
                    pe.wait_ge(*bank_free())
                    b = fill("xt", u, i, half).rearrange("p (k r) -> p k r", k=4)
                    for k in range(4):
                        ins = eng.transpose(b[:, k, 0:R], XN[0:R, i % 2, (4 * half + k) * 128:(4 * half + k + 1) * 128],
                                            ident[0:R, 0:R])
                    pe.did(ins.then_inc(pe_done, 1), "filled", "xt", u, i, half)

        def feature_major(w, label, mark):
            for part, c0, c1 in (("p", 0, SEQ), ("s", SEQ, TOK)):
                pe.wait_ge(*bank_free())
                b = fill(*label, part)
                for k in range(KT):
                    ins = mm(b[:, 0:c1 - c0], w[:, k * 128:(k + 1) * 128], XT[:, k, c0:c1],
                             start=(k == 0), stop=(k == KT - 1))
                pe.did(ins.then_inc(pe_done, 1), "filled", *label, part)
            counts.same(mark, ("filled",) + label + ("s",))

        def all_xt(u):
            for i in range(NT):
                pe.wait_ge(dve_done, at("drained", "xt", u, i, 1))

        def head_norm(L, i, kind, SQ):
            R = ROWS[i]
            pe.wait_ge(act_done, at(kind + "_sq", L, i))
            pe.wait_ge(*bank_free())
            b = fill(kind + "_ms", L, i).rearrange("p (c r) -> p c r", c=4)
            for c in range(2):
                ins = mm(b[:, c, 0:R], const("halves"), SQ[:, c, 0:R], start=True, stop=True)
            pe.did(ins.then_inc(pe_done, 1), "filled", kind + "_ms", L, i)

        for L in range(DEPTH):
            norm_turn(3 * L)
            all_xt(3 * L)
            for j in range(NFM):
                pe.wait_ge(sem(f"wf{j % NWF}_loaded"), at("wf", L, j))
                feature_major(WF[:, j % NWF, :], ("z", L, j), ("fm", L, j))
            pe.wait_ge(sem("wt_loaded"), at("wt", L))
            for i in range(NT):
                R = ROWS[i]
                pe.wait_ge(*bank_free())
                b = fill("zt", L, i)
                for k in range(KT):
                    ins = mm(b[0:R, 0:TMW], XT[:, k, COL[i]:COL[i] + R], WT[:, k, :], start=(k == 0), stop=(k == KT - 1))
                pe.did(ins.then_inc(pe_done, 1), "filled", "zt", L, i)
            counts.same(("w_in", L), ("filled", "zt", L, NT - 1))

            for what, src in (("cmean", CY), ("cvar", CQ)):
                for part, c0, c1 in (("p", 0, SEQ), ("s", SEQ, TOK)):
                    pe.wait_ge(*made(what + "_in", L))
                    pe.wait_ge(*bank_free())
                    b = fill(what, L, part)
                    for c in range(2):
                        ins = mm(b[:, 0:c1 - c0], ones, src[:, c, c0:c1], start=(c == 0), stop=(c == 1))
                    pe.did(ins.then_inc(pe_done, 1), "filled", what, L, part)
            pe.wait_ge(dve_done, at("pdiff", L))
            poolw = par("poolw").rearrange("p (c d) -> p c d", c=2)
            for c in range(2):
                for part, c0, c1 in (("p", 0, SEQ), ("s", SEQ, TOK)):
                    pe.wait_ge(*bank_free())
                    b = fill("py", L, c, part)
                    for hh in range(2):
                        r = slice(64 * hh, 64 * hh + 64)
                        ins = mm(b[r, 0:c1 - c0], poolw[r, c, :], CS[r, c, c0:c1], start=True, stop=True)
                    pe.did(ins.then_inc(pe_done, 1), "filled", "py", L, c, part)

            for i in range(NT):
                R, C = ROWS[i], ROWS[i] // CH
                cols = slice(COL[i], COL[i] + R)
                pe.wait_ge(dve_done, at("hkd", L))
                pe.wait_ge(*bank_free())
                b = fill("kdt", L, i)
                for c in range(2):
                    ins = eng.transpose(b[0:R, c * 128:(c + 1) * 128], KD[:, c, cols], ident)
                pe.did(ins.then_inc(pe_done, 1), "filled", "kdt", L, i)
                pe.wait_ge(act_done, at("drained", "kdt", L, i))
                pe.wait_ge(pool_done, at("vm", L, i))
                for c in range(2):
                    pe.wait_ge(*bank_free())
                    b = fill("hu", L, i, c)
                    for hh in range(2):
                        h = 2 * c + hh
                        ins = mm(b[64 * hh:64 * hh + 64, :], KDT[0:R, h * 64:(h + 1) * 64],
                                 VM[0:R, h].rearrange("p c v -> p (c v)"), start=True, stop=True)
                    pe.did(ins.then_inc(pe_done, 1), "filled", "hu", L, i, c)
                prod = PROD[:, 0:C * CH * C].rearrange("p (i s) -> p i s", i=C)
                for c in range(2):
                    pe.wait_ge(dve_done, at("prod", L, i, c))
                    pe.wait_ge(*bank_free())
                    b = fill("hsc", L, i, c)
                    for n in range(C):
                        ins = mm(b[0:R, 2 * n:2 * n + 2], prod[:, n, :], const("pair"), start=True, stop=True)
                    pe.did(ins.then_inc(pe_done, 1), "filled", "hsc", L, i, c)
                pe.wait_ge(dve_done, at("hst", L, i, 1))
                pe.wait_ge(*made(*(("hs", L) if i == SAMPLE else ("hstates", L, i))))
                pe.wait_ge(*bank_free())
                b = fill("ho", L, i).rearrange("p (c r) -> p c r", c=4)
                for h in range(4):
                    ins = mm(b[64 * (h % 2):64 * (h % 2) + 64, h // 2, 0:R], VT[0:R, i, h * 64:(h + 1) * 64],
                             ST[0:R, h, 0:R], start=(h < 2), stop=False, skip_group_check=True)
                row_tiles_change(ins)
                for c in range(2):
                    for hh in range(2):
                        r = slice(64 * hh, 64 * hh + 64)
                        for n in range(CH):
                            q = slice(COL[i] + n * C, COL[i] + (n + 1) * C)
                            ins = mm(b[r, c, n * C:(n + 1) * C], HS[r, c, n, :], LF[r, c, q], start=False,
                                     stop=(n == CH - 1), skip_group_check=True)
                pe.did(ins.then_inc(pe_done, 1), "filled", "ho", L, i)
                head_norm(L, i, "h", HSQ)

            for i in range(NT):
                R, S = ROWS[i], i == SAMPLE
                nb = NB if S else 1
                cols = slice(COL[i], COL[i] + R)
                suf = "_s" if S else "_p"
                tri = const("tri" + suf)
                pe.wait_ge(act_done, at("xc", L))
                for part, cs in ((0, (0, 1, 2, 3)), (1, (4, 5))):
                    pe.wait_ge(*bank_free())
                    b = fill("gt", L, i, part)
                    for n, c in enumerate(cs):
                        ins = eng.transpose(b[0:R, n * 128:(n + 1) * 128], XC[:, c, cols], ident)
                    pe.did(ins.then_inc(pe_done, 1), "filled", "gt", L, i, part)
                pe.wait_ge(dve_done, at("loga", L))
                pe.wait_ge(dve_done, at("logrows", L, i))
                loga = GSM[0:R, 4 * i:4 * i + 4]
                pe.wait_ge(*bank_free())
                b = fill("gg", L, i)
                mm(b[0:R, 0:4], tri[0:R, 0:R], loga, start=True, stop=True)
                mm(b[0:R, 4:8], (const("same_s") if S else ones)[0:R, 0:R], loga, start=True, stop=True)
                for c in range(2):
                    for hh in range(2):
                        h = 2 * c + hh
                        ins = mm(b[64 * hh:64 * hh + 64, 16 + c * nb:16 + (c + 1) * nb], ones[0:R, 0:64],
                                 GSM[0:R, 100 + h * nb:100 + (h + 1) * nb], start=True, stop=True)
                pe.did(ins.then_inc(pe_done, 1), "filled", "gg", L, i)
                pe.wait_ge(*bank_free())
                b = fill("gb", L, i).rearrange("p (h t) -> p h t", h=4)
                for h in range(4):
                    ins = mm(b[0:R, h, 0:R], LB[0:R, h, 0:R], tri[0:R, 0:R], start=True, stop=True)
                pe.did(ins.then_inc(pe_done, 1), "filled", "gb", L, i)
                pe.wait_ge(dve_done, at("qkn", L, i))
                for part in range(2):
                    pe.wait_ge(*bank_free())
                    b = fill("qkt", L, i, part).rearrange("p (c r) -> p c r", c=4)
                    srcs = ([QKN.rearrange("p a b -> p (a b)")[:, n * 128:(n + 1) * 128] for n in range(4)] if part == 0
                            else [QDN.rearrange("p a b -> p (a b)")[:, n * 128:(n + 1) * 128] for n in range(2)])
                    for n, src in enumerate(srcs):
                        ins = eng.transpose(b[:, n, 0:R], src[0:R, :], ident[0:R, 0:R])
                    pe.did(ins.then_inc(pe_done, 1), "filled", "qkt", L, i, part)
                pe.wait_ge(act_done, at("drained", "qkt", L, i, 0))
                banks = []
                for what in ("kk", "kq"):
                    pe.wait_ge(*bank_free())
                    banks.append(fill(what, L, i).rearrange("p (h t) -> p h t", h=4))
                for hh in range(2):
                    r = slice(64 * hh, 64 * hh + 64)
                    for what, b, right in (("kk", banks[0], 2), ("kq", banks[1], 0)):
                        for c in range(2):
                            ins = mm(b[0:R, 2 * c + hh, 0:R], QKT[r, 2 + c, 0:R], QKT[r, right + c, 0:R],
                                     start=True, stop=True)
                        if hh == 1:
                            pe.did(ins.then_inc(pe_done, 1), "filled", what, L, i)
                    if hh == 0:
                        row_tiles_change(ins)
                for l in range(LEVELS[S]):
                    last = l == LEVELS[S] - 1
                    pe.wait_ge(pool_done, at("am", L, i, l))
                    pe.wait_ge(dve_done, at("xi", L, i, l))
                    pe.wait_ge(*bank_free())
                    b = fill("pi", L, i, l).rearrange("p (h t) -> p h t", h=4)
                    for h in range(4):
                        ins = mm(b[0:R, h, 0:R], AM[0:R, l % 2, h, 0:R], XI[0:R, h, 0:R], start=True, stop=True)
                    pe.did(ins.then_inc(pe_done, 1), "filled", "pi", L, i, l)
                    pe.wait_ge(act_done, at("drained", "pi", L, i, l))
                    pe.wait_ge(*bank_free())
                    b = fill("dx", L, i, l).rearrange("p (h t) -> p h t", h=4)
                    for h in range(4):
                        ins = mm(b[0:R, h, 0:R], TI[0:R, h, 0:R], PI[0:R, h, 0:R], start=True, stop=True)
                    pe.did(ins.then_inc(pe_done, 1), "filled", "dx", L, i, l)
                    if not last:
                        pe.wait_ge(*bank_free())
                        b = fill("dt", L, i, l).rearrange("p (h t) -> p h t", h=4)
                        for h in range(4):
                            ins = mm(b[0:R, h, 0:R], PI[0:R, h, 0:R], TI[0:R, h, 0:R], start=True, stop=True)
                        pe.did(ins.then_inc(pe_done, 1), "filled", "dt", L, i, l)
                pe.wait_ge(dve_done, at("xi", L, i, LEVELS[S]))
                pe.wait_ge(dve_done, at("rhs", L, i))
                pe.wait_ge(*bank_free())
                b = fill("w2", L, i).rearrange("p (c r) -> p c r", c=4)
                for h in range(4):
                    ins = mm(b[64 * (h % 2):64 * (h % 2) + 64, h // 2, 0:R], RH2[0:R, h, :], XI[0:R, h, 0:R],
                             start=True, stop=True)
                pe.did(ins.then_inc(pe_done, 1), "filled", "w2", L, i)
                pe.wait_ge(act_done, at("drained", "w2", L, i))
                pe.wait_ge(*made(*(("gs", L) if S else ("gs_ready", L, i))))
                pe.wait_ge(*bank_free())
                b = fill("ut", L, i).rearrange("p (c r) -> p c r", c=4)
                w = R // nb
                for h in range(4):
                    r, c = slice(64 * (h % 2), 64 * (h % 2) + 64), h // 2
                    ins = mm(b[r, c, 0:R], RH1[0:R, h, :], XI[0:R, h, 0:R], start=(h < 2), stop=False,
                             skip_group_check=True)
                row_tiles_change(ins)
                for h in range(4):
                    r, c = slice(64 * (h % 2), 64 * (h % 2) + 64), h // 2
                    for n in range(nb):
                        ins = mm(b[r, c, n * w:(n + 1) * w], GS[r, c, n, :], W2T[r, c, n * w:(n + 1) * w],
                                 start=False, stop=(n == nb - 1), skip_group_check=True)
                pe.did(ins.then_inc(pe_done, 1), "filled", "ut", L, i)
                pe.wait_ge(act_done, at("drained", "ut", L, i))
                pe.wait_ge(*bank_free())
                b = fill("uu", L, i)
                for c in range(2):
                    ins = eng.transpose(b[0:R, c * 128:(c + 1) * 128], UT[:, c, 0:R], ident)
                pe.did(ins.then_inc(pe_done, 1), "filled", "uu", L, i)
                pe.wait_ge(act_done, at("drained", "qkt", L, i, 1))
                pe.wait_ge(dve_done, at("drained", "kq", L, i))
                pe.wait_ge(dve_done, at("drained", "uu", L, i))
                pe.wait_ge(*bank_free())
                b = fill("go", L, i).rearrange("p (c r) -> p c r", c=4)
                for h in range(4):
                    r, c = slice(64 * (h % 2), 64 * (h % 2) + 64), h // 2
                    ins = mm(b[r, c, 0:R], UU[0:R, h, :], DQ[0:R, h, 0:R], start=(h < 2), stop=False,
                             skip_group_check=True)
                row_tiles_change(ins)
                for h in range(4):
                    r, c = slice(64 * (h % 2), 64 * (h % 2) + 64), h // 2
                    for n in range(nb):
                        ins = mm(b[r, c, n * w:(n + 1) * w], GS[r, c, n, :], QKT[r, 4 + c, n * w:(n + 1) * w],
                                 start=False, stop=(n == nb - 1), skip_group_check=True)
                pe.did(ins.then_inc(pe_done, 1), "filled", "go", L, i)
                for c in range(2):
                    pe.wait_ge(*bank_free())
                    b = fill("gs", L, i, c)
                    for hh in range(2):
                        h = 2 * c + hh
                        rhs = UM[0:R, h].rearrange("p b v -> p (b v)") if S else UU[0:R, h, :]
                        ins = mm(b[64 * hh:64 * hh + 64, 0:nb * 64], KDEC[0:R, h, :], rhs, start=True, stop=True)
                    pe.did(ins.then_inc(pe_done, 1), "filled", "gs", L, i, c)
                head_norm(L, i, "g", GSQ)

            for kind in ("ha", "ga"):
                for i in range(NT):
                    pe.wait_ge(dve_done, at(kind, L, i))
            pe.wait_ge(act_done, at("cout", L))
            pe.wait_ge(act_done, at("pout", L))
            for k in range(0, KT, 2):
                pe.wait_ge(sem(f"wo{k}_loaded"), at("wo", L, k))
            for i in range(NT):
                R = ROWS[i]
                for half in range(2):
                    pe.wait_ge(*bank_free())
                    b = fill("wo", L, i, half)
                    for k in range(KT):
                        ins = mm(b[0:R, :], MIXT[:, k, COL[i]:COL[i] + R], WO[:, k, half * 512:(half + 1) * 512],
                                 start=(k == 0), stop=(k == KT - 1))
                    pe.did(ins.then_inc(pe_done, 1), "filled", "wo", L, i, half)

            norm_turn(3 * L + 1)
            all_xt(3 * L + 1)
            for j in range(KT):
                pe.wait_ge(sem(f"wf{j % NWF}_loaded"), at("wqload", L, j))
                feature_major(WQ[:, j % NWF, :], ("qt", L, j), ("wq", L, j))
            pe.wait_ge(sem("keys_loaded"), at("keys", L))

            def scores(i):
                R = ROWS[i]
                for g in range(4):
                    pe.wait_ge(*bank_free())
                    b = fill("sc", L, i, g)
                    p, r = g % 2, slice(64 * (g % 2), 64 * (g % 2) + 64)
                    for n in range(4):
                        h = 4 * (g // 2) + n
                        if i == 0 and p == 0:
                            pe.wait_ge(act_done, at("drained", "qt", L, h, "s"))
                        ins = mm(b[0:R, n * 128:(n + 1) * 128], QT[r, h, COL[i]:COL[i] + R], KEYS[r, h, :],
                                 start=True, stop=True)
                    pe.did(ins.then_inc(pe_done, 1), "filled", "sc", L, i, g)

            scores(0)
            scores(1)
            for i in range(NT):
                R = ROWS[i]
                pe.wait_ge(dve_done, at("igt", L, i))
                pe.wait_ge(*bank_free())
                b = fill("it", L, i).rearrange("p (c r) -> p c r", c=4)
                for c in range(3):
                    ins = eng.transpose(b[:, c, 0:R], IGT[0:R, c, :], ident[0:R, 0:R])
                pe.did(ins.then_inc(pe_done, 1), "filled", "it", L, i)
                if i + 2 < NT:
                    scores(i + 2)
            for n in range(max(fills["start"], fills["n"] - 8), fills["n"]):
                pe.wait_ge(*made("drained", *fills["order"][n]))
            with eng.Fori(0, NBLK) as b:
                for m in range(GBLK // 8):
                    batch = (b + NBLK * L) * 8 + m
                    eng.wait_ge(oh1_ready, batch + 2)
                    eng.wait_ge(oh2_ready, batch + 2)
                    for q in range(2):
                        eng.wait_ge(gates_copied, (b + NBLK * L) * 16 + (2 * m + q + 1))
                        for t in range(4):
                            ins = mm(PS[:, (m % 2) * 2 + q, t * 128:(t + 1) * 128], OH2[:, m % 2, 4 * q + t, :],
                                     OH1[:, m % 2, 4 * q + t, :], start=True, stop=True)
                        ins.then_inc(scattered, 1)
            eng.wait_ge(gates_copied, 16 * NBLK * (L + 1) + 4)

            pe.wait_ge(pool_done, at("xr", L))

            PARTS = ((0, 0), (1, 0), (0, 1))

            def u_rows(g, i):
                row = (g + NGROUPS * L) * GROUP + i
                eng.wait_ge(u_split, row + (2 * GROUP + 1))
                eng.wait_ge(gelu_done, row + 1)
                for part, c0, c1 in ((0, 0, HALF), (1, HALF, TOK)):
                    for k in range(KT):
                        for n, (a, b) in enumerate(PARTS):
                            ins = mm(PS[:, 2 * (i % 2) + part, 0:c1 - c0], UR[:, i, a, k * 128:(k + 1) * 128],
                                     XR[:, b, k, c0:c1], start=(k == 0 and n == 0), stop=(k == KT - 1 and n == 2))
                ins.then_inc(u_done, 1)

            def v_tiles(g, par_, d0, d1):
                for dt_ in range(d0, d1):
                    n_tile = (g + NGROUPS * L) * KT + dt_
                    eng.wait_ge(acc_done, n_tile + 1)
                    for part, c0, c1 in ((0, 0, HALF), (1, HALF, TOK)):
                        for r in range(GROUP):
                            for n, (a, b) in enumerate(PARTS):
                                ins = mm(PS[:, 4 + 2 * (dt_ % 2) + part, 0:c1 - c0],
                                         VR[:, par_ * GROUP + r, a, dt_ * 128:(dt_ + 1) * 128],
                                         HR[:, par_ * GROUP + r, b, c0:c1],
                                         start=(r == 0 and n == 0), stop=(r == GROUP - 1 and n == 2))
                    ins.then_inc(v_done, 1)

            for i in range(GROUP):
                u_rows(0, i)
            with eng.Fori(0, NGROUPS // 2 - 1) as it:
                for par_ in range(2):
                    g = it * 2 + par_
                    for i in range(GROUP):
                        u_rows(g + 1, i)
                        if i == 0:
                            eng.wait_ge(hm_done, (g + NGROUPS * L) * GROUP + GROUP + 2 * GROUP)
                            eng.wait_ge(v_split, (g + NGROUPS * L) * GROUP + GROUP + GROUP)
                        v_tiles(g, par_, TPR * i, TPR * (i + 1))
            for g in (NGROUPS - 2, NGROUPS - 1):
                for i in range(GROUP):
                    if g == NGROUPS - 2:
                        u_rows(g + 1, i)
                    if i == 0:
                        eng.wait_ge(hm_done, (g + NGROUPS * L) * GROUP + GROUP + 2 * GROUP)
                        eng.wait_ge(v_split, (g + NGROUPS * L) * GROUP + GROUP + GROUP)
                    v_tiles(g, g % 2, TPR * i, TPR * (i + 1))
            eng.wait_ge(gelu_done, NKEYS * (L + 1) + 2)
            eng.wait_ge(acc_done, KT * NGROUPS * (L + 1) + 2)
            fills["start"] = fills["n"]
            for i in range(NT):
                R = ROWS[i]
                for half in range(2):
                    pe.wait_ge(*bank_free())
                    b = fill("back", L, i, half)
                    for k in range(4):
                        ins = eng.transpose(b[0:R, k * 128:(k + 1) * 128], ACC[:, 4 * half + k, COL[i]:COL[i] + R], ident)
                    pe.did(ins.then_inc(pe_done, 1), "filled", "back", L, i, half)

            norm_turn(3 * L + 2)
            all_xt(3 * L + 2)
            for k in range(0, KT, 4):
                pe.wait_ge(sem(f"wg{k}_loaded"), at("wg", L, k))
            pe.wait_ge(sem("wp_loaded"), at("wp", L))
            pe.wait_ge(sem("pt_loaded"), at("pt", L))
            for i in range(NT):
                R = ROWS[i]
                cols = slice(COL[i], COL[i] + R)
                for half in range(2):
                    hs = slice(half * 512, (half + 1) * 512)
                    pe.wait_ge(*bank_free())
                    b = fill("pg", L, i, half)
                    for k in range(KT):
                        ins = mm(b[0:R, :], XT[:, k, cols], WG[:, k, hs], start=(k == 0), stop=(k == KT - 1))
                    pe.did(ins.then_inc(pe_done, 1), "filled", "pg", L, i, half)
                    pe.wait_ge(*bank_free())
                    b = fill("pp", L, i, half)
                    for k in range(2):
                        ins = mm(b[0:R, :], PT[:, k, cols], WP[:, k, hs], start=(k == 0), stop=(k == 1))
                    pe.did(ins.then_inc(pe_done, 1), "filled", "pp", L, i, half)

    @block.scalar
    def _(eng):
        act = Engine(eng, "act_done", counts)
        A = eng.activation

        def rms(u, i):
            R = ROWS[i]
            act.wait_ge(*(made("h", u, i) if u else made("x", i)))
            if i >= 2:
                if u == 3 * DEPTH:
                    act.wait_ge(*made("y_out", i - 2))
                else:
                    act.wait_ge(pe_done, at("filled", "xt", u, i - 2, 1))
            act.did(A(XN[0:R, i % 2, :], H[0:R, i, :], ACT.Square, accum_out=SS[0:R, i:i + 1]).then_inc(act_done, 1))
            act.wait_ge(act_done, count("act_done"))
            act.did(A(SS[0:R, 5 + i:6 + i], SS[0:R, i:i + 1], ACT.Sqrt, scale=1.0 / D, bias=const("eps")[0:R]).then_inc(act_done, 1), "rms", u, i)

        def copy_out(label, dst, src_part, func=ACT.Copy, **kw):
            act.wait_ge(pe_done, at("filled", *label))
            b = bank(*label)
            act.did(A(dst, src_part(b), func, **kw).then_inc(act_done, 1), "drained", *label)

        def head_norm(L, i, kind, SQ, RT):
            R = ROWS[i]
            act.wait_ge(pe_done, at("filled", kind + "o", L, i))
            b = bank(kind + "o", L, i).rearrange("p (c r) -> p c r", c=4)
            if i:
                act.wait_ge(pe_done, at("filled", kind + "_ms", L, i - 1))
            act.did(A(SQ[:, :, 0:R], b[:, 0:2, 0:R], ACT.Square).then_inc(act_done, 1), kind + "_sq", L, i)
            act.wait_ge(pe_done, at("filled", kind + "_ms", L, i))
            b = bank(kind + "_ms", L, i).rearrange("p (c r) -> p c r", c=4)
            if i:
                act.wait_ge(dve_done, at(kind + "a", L, i - 1))
            act.did(A(RT[:, :, 0:R], b[:, 0:2, 0:R], ACT.Sqrt, scale=1.0 / 64, bias=const("eps")).then_inc(act_done, 1), "drained", kind + "_ms", L, i)

        eng.sem_inc(gates_copied, 4)
        eng.sem_inc(gelu_done, 2)
        act.wait_ge(sem("const_loaded"), at("consts"))
        for L in range(DEPTH):
            for i in range(NT):
                rms(3 * L, i)
            if L:
                act.wait_ge(dve_done, at("lbx", L))
                act.did(A(LBV[:, 6:10], LBV[:, 6:10], ACT.Exp).then_inc(act_done, 1), "lbe", L)
            for j, name in enumerate(FM):
                c = int(name[-1])
                kind = name[:-1]
                if kind == "ca":
                    continue
                for part in "ps":
                    label = ("z", L, j, part)
                    act.wait_ge(pe_done, at("filled", *label))
                    b = bank(*label)
                    src = b[:, 0:SEQ] if part == "p" else bank_s(b)
                    pick = lambda t: t[:, c, 0:SEQ] if part == "p" else sam(t, c)
                    if kind == "cb":
                        act.did(A(pick(CS), src, ACT.Sigmoid).then_inc(act_done, 1), "drained", *label)
                    elif kind == "p":
                        dst = halo(PX, c, PW, POOLB, PWS) if part == "p" else halo_s(PX, c, PW, POOLB, PWS)
                        act.did(A(dst, src, ACT.Copy).then_inc(act_done, 1), "drained", *label)
                    elif kind == "k":
                        dst = halo(QR, c, QW, BCONV - 1, QWS) if part == "p" else halo_s(QR, c, QW, BCONV - 1, QWS)
                        act.did(A(dst, src, ACT.Copy).then_inc(act_done, 1), "drained", *label)
                    elif kind == "f":
                        act.did(A(pick(LF), src, ACT.Sigmoid).then_inc(act_done, 1))
                        act.did(A(pick(KF), src, ACT.Sigmoid, scale=-1.0).then_inc(act_done, 1), "drained", *label)
                    elif kind == "ga":
                        act.did(A(pick(GA), src, ACT.Sigmoid).then_inc(act_done, 1), "drained", *label)
                    elif kind == "q":
                        act.did(A(pick(ZQ), src, ACT.Silu).then_inc(act_done, 1), "drained", *label)
                    elif kind == "gb":
                        act.did(A(pick(GB), src, ACT.Silu).then_inc(act_done, 1), "drained", *label)
            for i in range(NT):
                R = ROWS[i]
                act.wait_ge(pe_done, at("filled", "zt", L, i))
                b = bank("zt", L, i)
                act.did(A(VT[0:R, i, :], b[0:R, 0:256], ACT.Copy).then_inc(act_done, 1))
                act.did(A(BA[0:R, i, :], b[0:R, 256:264], ACT.Copy).then_inc(act_done, 1), "drained", "zt", L, i)
            counts.same(("vt", L), ("drained", "zt", L, NT - 1))
            act.wait_ge(dve_done, at("cyc", L))
            act.did(A(CQ[:, :, :], CY[:, :, :], ACT.Square).then_inc(act_done, 1), "cvar_in", L)
            for part, c0, c1 in (("p", 0, SEQ), ("s", SEQ, TOK)):
                act.wait_ge(pe_done, at("filled", "cvar", L, part))
                b = bank("cvar", L, part)
                act.did(A(CQ[:, 0, c0:c1], b[:, 0:c1 - c0], ACT.Sqrt, scale=1.0 / 256, bias=const("eps")).then_inc(act_done, 1), "drained", "cvar", L, part)
            act.wait_ge(dve_done, at("cyn", L))
            for c in range(2):
                act.did(A(MIXT[:, 4 + c, :], CY[:, c, :], ACT.Silu, scale=par("cgain")[:, c:c + 1],
                          bias=par("cshift")[:, c:c + 1]).then_inc(act_done, 1), *(("cout", L) if c == 1 else ()))
            for c in range(2):
                for part, c0, c1 in (("p", 0, SEQ), ("s", SEQ, TOK)):
                    act.wait_ge(pe_done, at("filled", "py", L, c, part))
                    b = bank("py", L, c, part)
                    act.did(A(MIXT[:, 6 + c, c0:c1], b[:, 0:c1 - c0], ACT.Copy, scale=par("pscale")[:, c:c + 1]).then_inc(act_done, 1), "drained", "py", L, c, part)
            counts.same(("pout", L), ("drained", "py", L, 1, "s"))
            act.wait_ge(dve_done, at("hf", L))
            act.did(A(LF[:, :, :], LF[:, :, :], ACT.Ln).then_inc(act_done, 1), "hlog", L)
            act.wait_ge(dve_done, at("hla", L))
            act.did(A(EL[:, :, :], LA[:, :, :], ACT.Exp).then_inc(act_done, 1), "hel", L)
            act.wait_ge(dve_done, at("hdl", L))
            act.did(A(KD[:, :, :], KD[:, :, :], ACT.Exp).then_inc(act_done, 1), "hkde", L)
            act.wait_ge(dve_done, at("temps_free", L))
            for i in range(NT):
                R, C = ROWS[i], ROWS[i] // CH
                n = C * CH * C
                act.wait_ge(pe_done, at("filled", "kdt", L, i))
                b = bank("kdt", L, i)
                if i:
                    act.wait_ge(pe_done, at("filled", "hu", L, i - 1, 1))
                act.did(A(KDT[0:R, :], b[0:R, 0:256], ACT.Copy).then_inc(act_done, 1), "drained", "kdt", L, i)
                for c in range(2):
                    act.wait_ge(dve_done, at("hdiff", L, i, c))
                    act.did(A(PROD[:, 0:n], PROD[:, 0:n], ACT.Exp).then_inc(act_done, 1), "hexp", L, i, c)
                head_norm(L, i, "h", HSQ, HRT)
            act.wait_ge(dve_done, at("conv", L))
            for c in range(6):
                act.did(A(XC[:, c, :], XC[:, c, :], ACT.Silu).then_inc(act_done, 1), *(("xc", L) if c == 5 else ()))
            act.wait_ge(dve_done, at("dtx", L))
            act.did(A(GSM[:, 20:40], GSM[:, 20:40], ACT.Exp).then_inc(act_done, 1), "dte", L)
            act.wait_ge(dve_done, at("dte1", L))
            act.did(A(GSM[:, 20:40], GSM[:, 20:40], ACT.Ln).then_inc(act_done, 1), "dtl", L)
            act.did(A(GSM[:, 40:44], par("alog"), ACT.Exp).then_inc(act_done, 1), "ealog", L)
            act.did(A(GSM[:, 60:80].rearrange("p (i h) -> p i h", i=NT), BA[:, :, 0:4], ACT.Sigmoid).then_inc(act_done, 1), "beta", L)
            for i in range(NT):
                R, S = ROWS[i], i == SAMPLE
                nb = NB if S else 1
                act.wait_ge(pe_done, at("filled", "gt", L, i, 0))
                b = bank("gt", L, i, 0)
                if i:
                    act.wait_ge(dve_done, at("drained", "go", L, i - 1))
                act.did(A(LB[0:R].rearrange("p a b -> p (a b)"), b[0:R, :], ACT.Square).then_inc(act_done, 1), "qksq", L, i)
                act.wait_ge(dve_done, at("qkss", L, i))
                act.did(A(GSM[0:R, 80:88], GSM[0:R, 80:88], ACT.Sqrt, bias=const("eps")[0:R]).then_inc(act_done, 1), "qkrt", L, i)
                act.wait_ge(pe_done, at("filled", "gg", L, i))
                b = bank("gg", L, i)
                act.did(A(GSM[0:R, 44:48], b[0:R, 0:4], ACT.Exp).then_inc(act_done, 1))
                act.did(A(GSM[:, 132:132 + 2 * nb], b[:, 16:16 + 2 * nb], ACT.Exp).then_inc(act_done, 1), "eg", L, i)
                act.wait_ge(dve_done, at("gdl", L, i))
                act.did(A(GSM[0:R, 48:52], GSM[0:R, 48:52], ACT.Exp).then_inc(act_done, 1), "ekd", L, i)
                for h in range(4):
                    act.did(A(DA[0:R, h, 0:R], DA[0:R, h, 0:R], ACT.Exp, bias=GSM[0:R, 52 + h:53 + h]).then_inc(act_done, 1), *(("da", L, i) if h == 3 else ()))
                for h in range(4):
                    act.did(A(DQ[0:R, h, 0:R], DQ[0:R, h, 0:R], ACT.Exp, bias=GSM[0:R, 56 + h:57 + h]).then_inc(act_done, 1), *(("dq", L, i) if h == 3 else ()))
                for part, n0, n1 in ((0, 0, 4), (1, 4, 6)):
                    act.wait_ge(pe_done, at("filled", "qkt", L, i, part))
                    b = bank("qkt", L, i, part).rearrange("p (c r) -> p c r", c=4)
                    act.did(A(QKT[:, n0:n1, 0:R], b[:, 0:n1 - n0, 0:R], ACT.Copy).then_inc(act_done, 1), "drained", "qkt", L, i, part)
                for l in range(LEVELS[S]):
                    act.wait_ge(pe_done, at("filled", "pi", L, i, l))
                    b = bank("pi", L, i, l).rearrange("p (h t) -> p h t", h=4)
                    act.did(A(PI[0:R, :, 0:R], b[0:R, :, 0:R], ACT.Copy).then_inc(act_done, 1), "drained", "pi", L, i, l)
                act.wait_ge(pe_done, at("filled", "w2", L, i))
                b = bank("w2", L, i).rearrange("p (c r) -> p c r", c=4)
                act.did(A(W2T[:, :, 0:R], b[:, 0:2, 0:R], ACT.Copy, scale=-1.0).then_inc(act_done, 1), "drained", "w2", L, i)
                act.wait_ge(pe_done, at("filled", "ut", L, i))
                b = bank("ut", L, i).rearrange("p (c r) -> p c r", c=4)
                act.did(A(UT[:, :, 0:R], b[:, 0:2, 0:R], ACT.Copy).then_inc(act_done, 1), "drained", "ut", L, i)
                head_norm(L, i, "g", GSQ, GRT)
            for i in range(NT):
                rms(3 * L + 1, i)
            for j in range(KT):
                for part, c0, c1 in (("p", 0, SEQ), ("s", SEQ, TOK)):
                    act.wait_ge(pe_done, at("filled", "qt", L, j, part))
                    b = bank("qt", L, j, part)
                    act.did(A(QT[:, j, c0:c1], b[:, 0:c1 - c0], ACT.Copy).then_inc(act_done, 1), "drained", "qt", L, j, part)

            def scores(i):
                R = ROWS[i]
                if i >= 2:
                    act.wait_ge(dve_done, at("topk", L, i - 2))
                for g in range(4):
                    act.wait_ge(pe_done, at("filled", "sc", L, i, g))
                    b = bank("sc", L, i, g)
                    dst = SCO[0:R, i % 2, :].rearrange("p (h q n) -> p h q n", h=HEADS, q=2)
                    act.did(A(dst[:, 4 * (g // 2):4 * (g // 2) + 4, g % 2, :],
                              b[0:R, :].rearrange("p (h n) -> p h n", h=4), ACT.Copy).then_inc(act_done, 1), "drained", "sc", L, i, g)

            scores(0)
            scores(1)
            act.wait_ge(dve_done, at("drained", "xt", 3 * L + 1, NT - 1, 1))
            act.did(A(XR[:, 0], XT, ACT.Copy).then_inc(act_done, 1), "xr_high", L)
            for i in range(NT):
                R = ROWS[i]
                act.wait_ge(dve_done, at("gsub", L, i))
                act.did(A(IGT[0:R, 2, :], IGT[0:R, 2, :], ACT.Exp).then_inc(act_done, 1), "gexp", L, i)
                act.wait_ge(pe_done, at("filled", "it", L, i))
                b = bank("it", L, i).rearrange("p (c r) -> p c r", c=4)
                act.did(A(IT[:, :, COL[i]:COL[i] + R], b[:, 0:3, 0:R], ACT.Copy).then_inc(act_done, 1), "drained", "it", L, i)
                if i + 2 < NT:
                    scores(i + 2)
            with eng.Fori(0, NBLK // 3) as it:
                for j in range(3):
                    eng.wait_ge(d_gstore[j], (it + NBLK // 3 * L) * 16 + 16)
                    for n in range(16):
                        eng.wait_ge(scattered, (it * 3 + (j + NBLK * L)) * 16 + (n + 1 + 4))
                        A(GBUF[:, j, :, 4 * n:4 * n + 4], PS[:, n % 4, :].rearrange("p (t i) -> p i t", t=4),
                          ACT.Copy).then_inc(gates_copied, 1)

            def expert_rows(it, par_, more):
                g = it * 2 + par_
                for i in range(GROUP):
                    row = (g + NGROUPS * L) * GROUP + i
                    eng.wait_ge(d_v[i], (g + NGROUPS * L) * 16 + 16)
                    if i == 0:
                        eng.wait_ge(v_done, (g + NGROUPS * L) * KT + KT)
                    A(VR[:, par_ * GROUP + i, 0, :], VS[:, i, :], ACT.Copy).then_inc(v_rounded, 1)
                    eng.wait_ge(u_done, row + (1 + 2))
                    eng.wait_ge(hm_done, row + (1 + 2 * GROUP - 2))
                    A(GE[:, i % 2, :].rearrange("p (c t) -> p c t", c=2), PS[:, 2 * (i % 2):2 * (i % 2) + 2, 0:HALF],
                      ACT.Gelu).then_inc(gelu_done, 1)
                    if more:
                        slot = (1 - par_) * GROUP + i
                        eng.wait_ge(d_ut[slot], (it + (par_ + 1 + NGROUPS // 2 * L)) * 16)
                        A(UR[:, i, 0, :], US[:, slot, :], ACT.Copy).then_inc(u_rounded, 1)

            for i in range(GROUP):
                eng.wait_ge(d_ut[i], 16 * NGROUPS // 2 * L + 16)
                A(UR[:, i, 0, :], US[:, i, :], ACT.Copy).then_inc(u_rounded, 1)
            with eng.Fori(0, NGROUPS // 2 - 1) as it:
                for par_ in range(2):
                    expert_rows(it, par_, True)
            expert_rows(NGROUPS // 2 - 1, 0, True)
            expert_rows(NGROUPS // 2 - 1, 1, False)
            for i in range(NT):
                rms(3 * L + 2, i)
            for i in range(NT):
                R = ROWS[i]
                for half in range(2):
                    act.wait_ge(pe_done, at("filled", "pg", L, i, half))
                    b = bank("pg", L, i, half)
                    if i >= 2:
                        act.wait_ge(dve_done, at("drained", "pp", L, i - 2, half))
                    act.did(A(SG[0:R, i % 2, half * 512:(half + 1) * 512], b[0:R, :], ACT.Sigmoid).then_inc(act_done, 1), "drained", "pg", L, i, half)
        for i in range(NT):
            rms(3 * DEPTH, i)

    @block.gpsimd
    def _(eng):
        pool = Engine(eng, "pool_done", counts)
        eng.sem_inc(oh2_ready, 1)
        eng.sem_inc(u_split, 2 * GROUP)
        eng.sem_inc(v_split, GROUP)
        for L in range(DEPTH):
            if L:
                pool.wait_ge(dve_done, at("ple_done", L - 1))
            for c in range(2):
                pool.did(eng.memset(CU[:, c, 0:CCONV - 1], 0.0).then_inc(pool_done, 1))
                pool.did(eng.memset(PX[:, c, 0:POOLB], 0.0).then_inc(pool_done, 1))
            for c in range(6):
                pool.did(eng.memset(QR[:, c, 0:BCONV - 1], 0.0).then_inc(pool_done, 1))
            pool.wait_ge(pool_done, count("pool_done"))
            pool.did(eng.memset(BA[64:128, SAMPLE, :], 0.0).then_inc(pool_done, 1), "halos", L)
            pool.wait_ge(act_done, at("vt", L))
            pool.wait_ge(sem("const_loaded"), at("consts"))
            pool.wait_ge(dve_done, at("temps_free", L))
            for i in range(NT):
                R, C = ROWS[i], ROWS[i] // CH
                member = const("member_s" if i == SAMPLE else "member_p")
                if i:
                    pool.wait_ge(pe_done, at("filled", "hu", L, i - 1, 1))
                for h in range(4):
                    pool.did(eng.tensor_tensor(VM[0:R, h], bc(VT[0:R, i, h * 64:(h + 1) * 64], 1, CH),
                                               bc(member[0:R], 2, 64), ALU.mult).then_inc(pool_done, 1), *(("vm", L, i) if h == 3 else ()))
                if i == 0:
                    pool.wait_ge(dve_done, at("hk", L))
                    pool.wait_ge(act_done, at("drained", "z", L, FM.index("q1"), "s"))
                for c in range(2):
                    if i or c:
                        pool.wait_ge(dve_done, at("prod", L, *((i, 0) if c else (i - 1, 1))))
                    q = ZQ[:, c, COL[i]:COL[i] + R].rearrange("p (n t) -> p t n", n=CH)
                    k = KF[:, c, COL[i]:COL[i] + R].rearrange("p (n t) -> p n t", n=CH)
                    out = HQK[:, 0:C * CH * C].rearrange("p (i n s) -> p i n s", i=C, n=CH)
                    pool.did(eng.tensor_tensor(out, bc(q, 3, C), bc(k, 1, C), ALU.mult).then_inc(pool_done, 1), "hqk", L, i, c)
            for i in range(NT):
                R, S = ROWS[i], i == SAMPLE
                pool.wait_ge(dve_done, at("a", L, i))
                for l in range(LEVELS[S]):
                    if l >= 2:
                        pool.wait_ge(pe_done, at("filled", "pi", L, i, l - 2))
                    lev = const("levels")[0:R, l * 128:l * 128 + R]
                    pool.did(eng.tensor_tensor(AM[0:R, l % 2, :, 0:R], DA[0:R, :, 0:R], bc(lev, 1, 4), ALU.mult).then_inc(pool_done, 1), "am", L, i, l)
            pool.wait_ge(act_done, at("xr_high", L))
            pool.did(eng.tensor_tensor(XR[:, 1], XT, XR[:, 0].bitcast(F32), ALU.subtract).then_inc(pool_done, 1), "xr", L)
            with eng.Fori(0, NBLK) as b:
                eng.wait_ge(staged, b + NBLK * L + 1)
                for m in range(GBLK // 8):
                    eng.wait_ge(scattered, (b + NBLK * L) * 16 + (2 * m + 2))
                    eng.sem_inc(sem("oh2_begun"), 1)
                    for t in range(8):
                        ins = eng.tensor_scalar(OH2[:, m % 2, t, :], const("iota"),
                                                STG[:, 1, 8 * m + t:8 * m + t + 1], None, ALU.is_equal)
                    ins.then_inc(oh2_ready, 1)

            def low_parts(g, par_, more):
                for i in range(GROUP):
                    row = (g + NGROUPS * L) * GROUP + i
                    eng.wait_ge(v_rounded, row + 1)
                    eng.tensor_tensor(VR[:, par_ * GROUP + i, 1, :], VS[:, i, :],
                                      VR[:, par_ * GROUP + i, 0, :].bitcast(F32), ALU.subtract).then_inc(v_split, 1)
                    if more:
                        eng.wait_ge(u_rounded, row + (GROUP + 1))
                        eng.tensor_tensor(UR[:, i, 1, :], US[:, (1 - par_) * GROUP + i, :],
                                          UR[:, i, 0, :].bitcast(F32), ALU.subtract).then_inc(u_split, 1)

            for i in range(GROUP):
                eng.wait_ge(u_rounded, NKEYS * L + i + 1)
                eng.tensor_tensor(UR[:, i, 1, :], US[:, i, :], UR[:, i, 0, :].bitcast(F32), ALU.subtract)\
                    .then_inc(u_split, 1)
            with eng.Fori(0, NGROUPS // 2 - 1) as it:
                for par_ in range(2):
                    low_parts(it * 2 + par_, par_, True)
            low_parts(NGROUPS - 2, 0, True)
            low_parts(NGROUPS - 1, 1, False)

    @block.vector
    def _(eng):
        dve = Engine(eng, "dve_done", counts)
        TT, TS, STT = eng.tensor_tensor, eng.tensor_scalar, eng.scalar_tensor_tensor

        def norm(u):
            def scale(i):
                R = ROWS[i]
                dve.wait_ge(act_done, at("rms", u, i))
                dve.did(eng.reciprocal(SS[0:R, 10 + i:11 + i], SS[0:R, 5 + i:6 + i]).then_inc(dve_done, 1))
                dve.wait_ge(dve_done, count("dve_done"))
                dve.did(TS(XN[0:R, i % 2, :], H[0:R, i, :], SS[0:R, 10 + i:11 + i], None, ALU.mult).then_inc(dve_done, 1), "xn", u, i)

            def turned(i):
                R = ROWS[i]
                gain = par("gain")[:, (u % 3) * 8:(u % 3) * 8 + 8]
                for half in range(2):
                    dve.wait_ge(pe_done, at("filled", "xt", u, i, half))
                    b = bank("xt", u, i, half).rearrange("p (k r) -> p k r", k=4)
                    dve.did(TT(XT[:, 4 * half:4 * half + 4, COL[i]:COL[i] + R], b[:, :, 0:R],
                               bc(gain[:, 4 * half:4 * half + 4], 2, R), ALU.mult).then_inc(dve_done, 1), "drained", "xt", u, i, half)

            for i in range(NT):
                scale(i)
                if i:
                    turned(i - 1)
            turned(NT - 1)

        def head_out(L, i, kind, RT, ON, gate, w, k0):
            R = ROWS[i]
            cols = slice(COL[i], COL[i] + R)
            dve.wait_ge(act_done, at("drained", kind + "_ms", L, i))
            dve.did(eng.reciprocal(RT[:, :, 0:R], RT[:, :, 0:R]).then_inc(dve_done, 1))
            dve.wait_ge(dve_done, count("dve_done"))
            dve.wait_ge(pe_done, at("filled", kind + "o", L, i))
            b = bank(kind + "o", L, i).rearrange("p (c r) -> p c r", c=4)
            dve.did(TT(ON[:, :, 0:R], b[:, 0:2, 0:R], RT[:, :, 0:R], ALU.mult).then_inc(dve_done, 1), "drained", kind + "o", L, i)
            dve.wait_ge(dve_done, count("dve_done"))
            for c in range(2):
                dve.did(STT(MIXT[:, k0 + c, cols], ON[:, c, 0:R], w[:, c:c + 1], gate[:, c, cols], ALU.mult, ALU.mult).then_inc(dve_done, 1), *((kind + "a", L, i) if c == 1 else ()))

        def add_h(L, i, half, label, u):
            R = ROWS[i]
            dve.wait_ge(pe_done, at("filled", label, L, i, half))
            b = bank(label, L, i, half)
            hs = H[0:R, i, half * 512:(half + 1) * 512]
            dve.did(TT(hs, hs, b[0:R, :], ALU.add).then_inc(dve_done, 1), "drained", label, L, i, half)
            if half == 1:
                counts.same(("h", u, i), ("drained", label, L, i, half))

        eng.sem_inc(hm_done, 2 * GROUP)
        eng.sem_inc(acc_done, 2)
        eng.sem_inc(oh1_ready, 1)
        dve.wait_ge(sem("const_loaded"), at("consts"))
        dve.wait_ge(sem("params_loaded"), at("params", 0))
        lg = par("logits")
        for L in range(DEPTH):
            if L:
                dve.wait_ge(sem("params_loaded"), at("params", L))
            norm(3 * L)
            if L == 0:
                dve.did(eng.memset(LBV[:, 0:2], 0.0).then_inc(dve_done, 1))
                dve.wait_ge(dve_done, count("dve_done"))
                dve.did(TS(LBV[:, 2:4], LBV[:, 0:2], -1.0, 1.0, ALU.mult, ALU.add).then_inc(dve_done, 1), "lb", L)
            else:
                dve.did(TT(LBV[:, 4:6], lg[:, 0:2], lg[:, 2:4], ALU.max).then_inc(dve_done, 1))
                dve.wait_ge(dve_done, count("dve_done"))
                dve.did(TT(LBV[:, 6:8], lg[:, 0:2], LBV[:, 4:6], ALU.subtract).then_inc(dve_done, 1))
                dve.did(TT(LBV[:, 8:10], lg[:, 2:4], LBV[:, 4:6], ALU.subtract).then_inc(dve_done, 1), "lbx", L)
                dve.wait_ge(act_done, at("lbe", L))
                dve.did(TT(LBV[:, 4:6], LBV[:, 6:8], LBV[:, 8:10], ALU.add).then_inc(dve_done, 1))
                dve.wait_ge(dve_done, count("dve_done"))
                dve.did(eng.reciprocal(LBV[:, 10:12], LBV[:, 4:6]).then_inc(dve_done, 1))
                dve.wait_ge(dve_done, count("dve_done"))
                dve.did(TT(LBV[:, 0:2], LBV[:, 8:10], LBV[:, 10:12], ALU.mult).then_inc(dve_done, 1))
                dve.wait_ge(dve_done, count("dve_done"))
                dve.did(TS(LBV[:, 2:4], LBV[:, 0:2], -1.0, 1.0, ALU.mult, ALU.add).then_inc(dve_done, 1), "lb", L)

            dve.wait_ge(pool_done, at("halos", L))
            for c in range(2):
                ja, jb = FM.index(f"ca{c}"), FM.index(f"cb{c}")
                for part in "ps":
                    dve.wait_ge(act_done, at("drained", "z", L, jb, part))
                    dve.wait_ge(pe_done, at("filled", "z", L, ja, part))
                    b = bank("z", L, ja, part)
                    if part == "p":
                        ins = TT(halo(CU, c, CW, CCONV - 1, CWS), b[:, 0:SEQ], CS[:, c, 0:SEQ], ALU.mult)
                    else:
                        ins = TT(halo_s(CU, c, CW, CCONV - 1, CWS), bank_s(b), sam(CS, c), ALU.mult)
                    dve.did(ins.then_inc(dve_done, 1), "drained", "z", L, ja, part)
                counts.same(("cu_ready", L, c), ("drained", "z", L, ja, "s"))
            for c in range(2):
                dve.wait_ge(sem(f"cu{c}_loaded"), at("cu", L, c))
            dve.wait_ge(dve_done, count("dve_done"))
            for j in range(CCONV):
                for c in range(2):
                    w = par("cconv")[:, c * CCONV + j:c * CCONV + j + 1]
                    for out, src in ((CY[:, c, 0:SEQ], CU[:, c, j:j + SEQ]),
                                     (sam(CY, c), CU[:, c, CW:].rearrange("p (b w) -> p b w", b=NB)[:, :, j:j + NS])):
                        if j == 0:
                            dve.did(TS(out, src, w, par("cbias")[:, c:c + 1], ALU.mult, ALU.add).then_inc(dve_done, 1))
                        else:
                            dve.did(STT(out, src, w, out, ALU.mult, ALU.add).then_inc(dve_done, 1), *(("cmean_in", L) if (j, c) == (CCONV - 1, 1) and out.shape[-1] == NS else ()))
                dve.wait_ge(dve_done, count("dve_done"))
            for c in range(2):
                for part in "ps":
                    dve.wait_ge(act_done, at("drained", "z", L, FM.index(f"p{c}"), part))
                dve.wait_ge(sem(f"px{c}_loaded"), at("px", L, c))
            PXS = lambda t, a, b, r=slice(0, 128), c=slice(0, 2): t[r, c, a:b]
            PSS = lambda t, c, a, b, r=slice(0, 128): t[r, c, PW:].rearrange("p (b w) -> p b w", b=NB)[:, :, a:b]
            steps = [(PX, PA, 1), (PA, PB, 2), (PB, PA, 4), (PA, PB, 8)]
            for n, (src, dst, by) in enumerate(steps):
                lo = 2 * by - 1
                for c in range(2):
                    if n >= 2 and c == 0:
                        continue
                    dve.did(TT(dst[:, c, lo:PW], src[:, c, lo:PW], src[:, c, lo - by:PW - by], ALU.add).then_inc(dve_done, 1))
                    dve.did(TT(PSS(dst, c, lo, PWS), PSS(src, c, lo, PWS), PSS(src, c, lo - by, PWS - by), ALU.add).then_inc(dve_done, 1))
                dve.wait_ge(dve_done, count("dve_done"))
                c, r = n // 2, slice(64 * (n % 2), 64 * (n % 2) + 64)
                ic = const("inv_count")[r, 16 * c:16 * c + 16]
                iw = const("inv_window")[r, c:c + 1]
                dve.did(TT(CS[r, c, 0:16], dst[r, c, POOLB:POOLB + 16], ic, ALU.mult).then_inc(dve_done, 1))
                dve.wait_ge(dve_done, count("dve_done"))
                dve.did(TT(CS[r, c, 0:16], CS[r, c, 0:16], PX[r, c, POOLB:POOLB + 16], ALU.subtract).then_inc(dve_done, 1))
                dve.did(STT(CS[r, c, 16:SEQ], dst[r, c, POOLB + 16:PW], iw, PX[r, c, POOLB + 16:PW],
                            ALU.mult, ALU.subtract).then_inc(dve_done, 1))
                dve.did(STT(CS[r, c, SEQ:TOK].rearrange("p (b w) -> p b w", b=NB), PSS(dst, c, POOLB, PWS, r), iw,
                            PSS(PX, c, POOLB, PWS, r), ALU.mult, ALU.subtract).then_inc(dve_done, 1), *(("pdiff", L) if n == 3 else ()))
            for c in range(2):
                counts.same(("px_ready", L, c), ("pdiff", L))
            for part, c0, c1 in (("p", 0, SEQ), ("s", SEQ, TOK)):
                dve.wait_ge(pe_done, at("filled", "cmean", L, part))
                b = bank("cmean", L, part)
                for c in range(2):
                    ins = STT(CY[:, c, c0:c1], b[:, 0:c1 - c0], -1.0 / 256, CY[:, c, c0:c1], ALU.mult, ALU.add)
                    dve.did(ins.then_inc(dve_done, 1), *(("drained", "cmean", L, part) if c else ()))
            counts.same(("cyc", L), ("drained", "cmean", L, "s"))
            for part in "ps":
                dve.wait_ge(act_done, at("drained", "cvar", L, part))
            dve.did(eng.reciprocal(CQ[:, 1, :], CQ[:, 0, :]).then_inc(dve_done, 1))
            dve.wait_ge(dve_done, count("dve_done"))
            dve.did(TT(CY[:, :, :], CY[:, :, :], bc(CQ[:, 1, :], 1, 2), ALU.mult).then_inc(dve_done, 1), "cyn", L)

            for name in ("f0", "f1"):
                for part in "ps":
                    dve.wait_ge(act_done, at("drained", "z", L, FM.index(name), part))
            for c in range(2):
                dve.did(TS(LF[:, c, :], LF[:, c, :], LBV[:, 2 + c:3 + c], LBV[:, c:c + 1], ALU.mult, ALU.add).then_inc(dve_done, 1))
                dve.did(TS(KF[:, c, :], KF[:, c, :], LBV[:, 2 + c:3 + c], None, ALU.mult).then_inc(dve_done, 1), *(("hk", L) if c else ()))
            dve.wait_ge(dve_done, count("dve_done"))
            dve.did(TS(LF[:, :, :], LF[:, :, :], F_MIN, None, ALU.max).then_inc(dve_done, 1), "hf", L)
            for c in range(6):
                for part in "ps":
                    dve.wait_ge(act_done, at("drained", "z", L, FM.index(f"k{c}"), part))
                dve.wait_ge(sem(f"qr{c}_loaded"), at("qr", L, c))
            dve.wait_ge(pe_done, at("w_in", L))
            if L:
                dve.wait_ge(sem("gs_s_stored"), at("gs2_out", L - 1))
            for j in range(BCONV):
                for c in range(6):
                    w = par("qconv")[:, c * BCONV + j:c * BCONV + j + 1]
                    for out, src in ((XC[:, c, 0:SEQ], QR[:, c, j:j + SEQ]),
                                     (sam(XC, c), QR[:, c, QW:].rearrange("p (b w) -> p b w", b=NB)[:, :, j:j + NS])):
                        if j == 0:
                            ins = TS(out, src, w, None, ALU.mult)
                        else:
                            ins = STT(out, src, w, out, ALU.mult, ALU.add)
                        dve.did(ins.then_inc(dve_done, 1), *(("conv", L) if (j, c) == (BCONV - 1, 5) and out.shape[-1] == NS else ()))
                dve.wait_ge(dve_done, count("dve_done"))
            for c in range(6):
                counts.same(("qr_ready", L, c), ("conv", L))
            dve.wait_ge(act_done, at("hlog", L))
            for c in range(2):
                dve.did(eng.tensor_tensor_scan(LA[:, c, :], const("carry"), LF[:, c, :], 0.0, ALU.mult, ALU.add).then_inc(dve_done, 1), *(("hla", L) if c else ()))
            dve.wait_ge(dve_done, count("dve_done"))
            for c in range(2):
                for c0, c1, n in ((0, SEQ, SEQ // 16), (SEQ, TOK, NB)):
                    la = LA[:, c, c0:c1].rearrange("p (n t) -> p n t", n=n)
                    w = (c1 - c0) // n
                    dve.did(TT(KD[:, c, c0:c1].rearrange("p (n t) -> p n t", n=n),
                               la[:, :, w - 1:w].broadcast_to([128, n, w]), la, ALU.subtract).then_inc(dve_done, 1), *(("hdl", L) if (c, c0) == (1, SEQ) else ()))
            dve.wait_ge(act_done, at("hel", L))
            for name in ("q0", "q1"):
                for part in "ps":
                    dve.wait_ge(act_done, at("drained", "z", L, FM.index(name), part))
            dve.did(TT(LF[:, :, :], ZQ[:, :, :], EL[:, :, :], ALU.mult).then_inc(dve_done, 1), "hqd", L)
            dve.wait_ge(act_done, at("hkde", L))
            dve.did(TT(KD[:, :, :], KD[:, :, :], KF[:, :, :], ALU.mult).then_inc(dve_done, 1), "hkd", L)
            dve.wait_ge(act_done, at("cout", L))
            dve.wait_ge(act_done, at("pout", L))
            dve.wait_ge(sem("conf_stored"), at("conf_out", L, 1))
            dve.wait_ge(sem("pool_stored"), at("pool_out", L, 1))
            dve.did(eng.memset(HS[:, :, 0, :], 0.0).then_inc(dve_done, 1), "temps_free", L)
            for i in range(NT):
                R, C = ROWS[i], ROWS[i] // CH
                S = i == SAMPLE
                n = C * CH * C
                cols = slice(COL[i], COL[i] + R)
                for c in range(2):
                    la = LA[:, c, cols].rearrange("p (n t) -> p n t", n=CH)
                    lat = LA[:, c, cols].rearrange("p (n t) -> p t n", n=CH)
                    prod = PROD[:, 0:n].rearrange("p (i n s) -> p i n s", i=C, n=CH)
                    if i or c:
                        dve.wait_ge(pe_done, at("filled", "hsc", L, *((i, 0) if c else (i - 1, 1))))
                    dve.did(TT(prod, bc(lat, 3, C), bc(la, 1, C), ALU.subtract).then_inc(dve_done, 1))
                    dve.wait_ge(dve_done, count("dve_done"))
                    dve.did(TS(PROD[:, 0:n], PROD[:, 0:n], 0.0, None, ALU.min).then_inc(dve_done, 1), "hdiff", L, i, c)
                    if c == 0:
                        for cc in range(2):
                            dve.wait_ge(pe_done, at("filled", "hu", L, i, cc))
                            b = bank("hu", L, i, cc).rearrange("p (n v) -> p n v", n=CH)
                            tot = EL[:, cc, cols].rearrange("p (n t) -> p n t", n=CH)[:, :, C - 1]
                            if S:
                                continue
                            for m in range(CH):
                                dve.did(STT(HS[:, cc, m + 1, :], HS[:, cc, m, :], tot[:, m:m + 1], b[:, m, :],
                                            ALU.mult, ALU.add).then_inc(dve_done, 1), *(("drained", "hu", L, i, cc) if m == CH - 1 else ()))
                                dve.wait_ge(dve_done, count("dve_done"))
                        if not S:
                            counts.same(("hstates", L, i), ("drained", "hu", L, i, 1))
                    dve.wait_ge(act_done, at("hexp", L, i, c))
                    dve.wait_ge(pool_done, at("hqk", L, i, c))
                    dve.did(TT(PROD[:, 0:n], PROD[:, 0:n], HQK[:, 0:n], ALU.mult).then_inc(dve_done, 1), "prod", L, i, c)
                    dve.wait_ge(pe_done, at("filled", "hsc", L, i, c))
                    b = bank("hsc", L, i, c)
                    if i:
                        dve.wait_ge(pe_done, at("filled", "ho", L, i - 1))
                    sc = b[0:R, 0:2 * C].rearrange("p (i h) -> p h i", h=2)
                    mask = const("chunk_s" if S else "chunk_p")[0:R, 0:R].rearrange("p (n i) -> p n i", n=CH)
                    for hh in range(2):
                        out = ST[0:R, 2 * c + hh, 0:R].rearrange("p (n i) -> p n i", n=CH)
                        dve.did(TT(out, bc(sc[:, hh, :], 1, CH), mask, ALU.mult).then_inc(dve_done, 1), *(("hst", L, i, c) if hh else ()))
                    counts.same(("drained", "hsc", L, i, c), ("hst", L, i, c))
                head_out(L, i, "h", HRT, HON, GA, par("hnorm"), 0)
                if i < SAMPLE:
                    dve.wait_ge(pe_done, at("filled", "ho", L, i))
                    dve.did(eng.tensor_copy(HS[:, :, 0, :], HS[:, :, CH, :]).then_inc(dve_done, 1), *(("hs_prompt", L) if i == SAMPLE - 1 else ()))
                    dve.wait_ge(dve_done, count("dve_done"))
                else:
                    dve.wait_ge(pe_done, at("filled", "ho", L, i))
                    for cc in range(2):
                        dve.wait_ge(pe_done, at("filled", "hu", L, i, cc))
                        b = bank("hu", L, i, cc).rearrange("p (n v) -> p n v", n=CH)
                        tot = EL[:, cc, cols].rearrange("p (n t) -> p n t", n=CH)[:, :, C - 1]
                        dve.did(TT(HS[:, cc, 0:NB, :], HS[:, cc, 0:NB, :], bc(tot, 2, 64), ALU.mult).then_inc(dve_done, 1))
                        dve.wait_ge(dve_done, count("dve_done"))
                        dve.did(TT(HS[:, cc, 0:NB, :], HS[:, cc, 0:NB, :], b, ALU.add).then_inc(dve_done, 1), "drained", "hu", L, i, cc)
                    counts.same(("hs_sample", L), ("drained", "hu", L, i, 1))

            dve.wait_ge(sem("hs_s_stored"), at("hs2_out", L))
            x = GSM[:, 0:20].rearrange("p (i h) -> p i h", i=NT)
            dve.wait_ge(act_done, at("vt", L))
            dve.did(TT(x, BA[:, :, 4:8], bc(par("dt"), 1, NT), ALU.add).then_inc(dve_done, 1))
            dve.wait_ge(dve_done, count("dve_done"))
            dve.did(TS(GSM[:, 20:40], GSM[:, 0:20], -1.0, None, ALU.mult).then_inc(dve_done, 1))
            dve.wait_ge(dve_done, count("dve_done"))
            dve.did(TT(GSM[:, 20:40], GSM[:, 20:40], GSM[:, 0:20], ALU.min).then_inc(dve_done, 1), "dtx", L)
            dve.wait_ge(act_done, at("dte", L))
            dve.did(TS(GSM[:, 20:40], GSM[:, 20:40], 1.0, None, ALU.add).then_inc(dve_done, 1), "dte1", L)
            dve.wait_ge(act_done, at("dtl", L))
            dve.did(STT(GSM[:, 0:20], GSM[:, 0:20], 0.0, GSM[:, 20:40], ALU.max, ALU.add).then_inc(dve_done, 1))
            dve.wait_ge(dve_done, count("dve_done"))
            dve.wait_ge(act_done, at("ealog", L))
            dve.did(STT(x, x, -1.0, bc(GSM[:, 40:44], 1, NT), ALU.mult, ALU.mult).then_inc(dve_done, 1), "loga", L)
            dve.did(eng.memset(GS[:, :, 0, :], 0.0).then_inc(dve_done, 1))
            dve.wait_ge(dve_done, count("dve_done"))
            counts.marks[("gs_ready", L, 0)] = ("dve_done", count("dve_done"))
            for i in range(NT):
                R, S = ROWS[i], i == SAMPLE
                nb = NB if S else 1
                suf = "_s" if S else "_p"
                loga = GSM[0:R, 4 * i:4 * i + 4]
                beta = GSM[0:R, 60 + 4 * i:64 + 4 * i]
                dve.wait_ge(act_done, at("qksq", L, i))
                dve.did(eng.tensor_reduce(GSM[0:R, 80:88],
                                          LB[0:R].rearrange("p a b -> p (a b)").rearrange("p (h d) -> p h d", h=8),
                                          AX, ALU.add).then_inc(dve_done, 1), "qkss", L, i)
                dve.wait_ge(dve_done, count("dve_done"))
                dve.did(TT(LB[0:R, :, 0:R], bc(ones[0:R, 0:R], 1, 4), bc(loga, 2, R), ALU.mult).then_inc(dve_done, 1))
                if S:
                    ins = TT(GSM[0:R, 100:100 + 4 * nb].rearrange("p (h b) -> p h b", h=4),
                             bc(loga, 2, nb), bc(const("member_s")[0:R], 1, 4), ALU.mult)
                else:
                    ins = eng.tensor_copy(GSM[0:R, 100:104], loga)
                dve.did(ins.then_inc(dve_done, 1), "logrows", L, i)
                dve.wait_ge(act_done, at("qkrt", L, i))
                dve.did(eng.reciprocal(GSM[0:R, 88:96], GSM[0:R, 80:88]).then_inc(dve_done, 1))
                dve.wait_ge(dve_done, count("dve_done"))
                dve.did(TS(GSM[0:R, 88:92], GSM[0:R, 88:92], 64.0 ** -0.5, None, ALU.mult).then_inc(dve_done, 1))
                dve.wait_ge(dve_done, count("dve_done"))
                dve.wait_ge(pe_done, at("filled", "gt", L, i, 0))
                b = bank("gt", L, i, 0).rearrange("p (h d) -> p h d", h=8)
                dve.did(TT(QKN[0:R], b[0:R], bc(GSM[0:R, 88:96], 2, 64), ALU.mult).then_inc(dve_done, 1), "drained", "gt", L, i, 0)
                dve.wait_ge(act_done, at("beta", L))
                dve.wait_ge(pe_done, at("filled", "gt", L, i, 1))
                b = bank("gt", L, i, 1).rearrange("p (h d) -> p h d", h=8)
                dve.did(TT(RH1[0:R], b[0:R, 0:4], bc(beta, 2, 64), ALU.mult).then_inc(dve_done, 1), "drained", "gt", L, i, 1)
                dve.wait_ge(act_done, at("eg", L, i))
                dve.wait_ge(dve_done, count("dve_done"))
                eg = GSM[0:R, 44:48]
                dve.did(TT(QDN[0:R], QKN[0:R, 0:4], bc(eg, 2, 64), ALU.mult).then_inc(dve_done, 1), "qkn", L, i)
                dve.did(TT(GSM[0:R, 96:100], eg, beta, ALU.mult).then_inc(dve_done, 1))
                dve.wait_ge(pe_done, at("filled", "gg", L, i))
                b = bank("gg", L, i)
                dve.did(eng.tensor_copy(GSM[0:R, 52:56], b[0:R, 0:4]).then_inc(dve_done, 1))
                dve.wait_ge(dve_done, count("dve_done"))
                dve.did(TS(GSM[0:R, 56:60], GSM[0:R, 52:56], -1.0, None, ALU.mult).then_inc(dve_done, 1))
                dve.did(TT(GSM[0:R, 48:52], b[0:R, 4:8], GSM[0:R, 52:56], ALU.subtract).then_inc(dve_done, 1), "drained", "gg", L, i)
                dve.did(TT(RH2[0:R], QKN[0:R, 4:8], bc(GSM[0:R, 96:100], 2, 64), ALU.mult).then_inc(dve_done, 1), "rhs", L, i)
                dve.wait_ge(pe_done, at("filled", "gb", L, i))
                b = bank("gb", L, i).rearrange("p (h t) -> p h t", h=4)
                below = bc(const("below" + suf)[0:R, 0:R], 1, 4)
                upto = bc(const("upto" + suf)[0:R, 0:R], 1, 4)
                dve.did(STT(DA[0:R, :, 0:R], b[0:R, :, 0:R], -1.0, below, ALU.mult, ALU.add).then_inc(dve_done, 1))
                dve.did(TT(DQ[0:R, :, 0:R], b[0:R, :, 0:R], upto, ALU.add).then_inc(dve_done, 1), "drained", "gb", L, i)
                counts.same(("gdl", L, i), ("drained", "gb", L, i))
                dve.did(eng.tensor_copy(XI[0:R, :, 0:R], bc(ident[0:R, 0:R], 1, 4)).then_inc(dve_done, 1))
                dve.did(eng.tensor_copy(TI[0:R, :, 0:R], bc(ident[0:R, 0:R], 1, 4)).then_inc(dve_done, 1), "xi", L, i, 0)
                dve.wait_ge(act_done, at("ekd", L, i))
                dve.did(TT(KDEC[0:R], QKN[0:R, 4:8], bc(GSM[0:R, 48:52], 2, 64), ALU.mult).then_inc(dve_done, 1))
                dve.wait_ge(act_done, at("da", L, i))
                dve.wait_ge(pe_done, at("filled", "kk", L, i))
                b = bank("kk", L, i).rearrange("p (h t) -> p h t", h=4)
                dve.did(TT(DA[0:R, :, 0:R], DA[0:R, :, 0:R], b[0:R, :, 0:R], ALU.mult).then_inc(dve_done, 1), "drained", "kk", L, i)
                dve.wait_ge(dve_done, count("dve_done"))
                dve.did(TT(DA[0:R, :, 0:R], DA[0:R, :, 0:R], bc(beta, 2, R), ALU.mult).then_inc(dve_done, 1), "a", L, i)
                dve.wait_ge(act_done, at("dq", L, i))
                dve.wait_ge(pe_done, at("filled", "kq", L, i))
                b = bank("kq", L, i).rearrange("p (h t) -> p h t", h=4)
                dve.did(TT(DQ[0:R, :, 0:R], DQ[0:R, :, 0:R], b[0:R, :, 0:R], ALU.mult).then_inc(dve_done, 1), "drained", "kq", L, i)
                for l in range(LEVELS[S]):
                    last = l == LEVELS[S] - 1
                    dve.wait_ge(pe_done, at("filled", "dx", L, i, l))
                    b = bank("dx", L, i, l).rearrange("p (h t) -> p h t", h=4)
                    dve.did(TT(XI[0:R, :, 0:R], XI[0:R, :, 0:R], b[0:R, :, 0:R], ALU.subtract).then_inc(dve_done, 1), "drained", "dx", L, i, l)
                    if not last:
                        dve.wait_ge(pe_done, at("filled", "dt", L, i, l))
                        b = bank("dt", L, i, l).rearrange("p (h t) -> p h t", h=4)
                        dve.did(TT(TI[0:R, :, 0:R], TI[0:R, :, 0:R], b[0:R, :, 0:R], ALU.subtract).then_inc(dve_done, 1), "drained", "dt", L, i, l)
                    dve.wait_ge(dve_done, count("dve_done"))
                    counts.marks[("xi", L, i, l + 1)] = ("dve_done", count("dve_done"))
                dve.wait_ge(pe_done, at("filled", "uu", L, i))
                b = bank("uu", L, i).rearrange("p (h v) -> p h v", h=8)
                if S:
                    for h in range(4):
                        dve.did(TT(UM[0:R, h], bc(b[0:R, h, :], 1, NB), bc(const("member_s")[0:R], 2, 64), ALU.mult).then_inc(dve_done, 1))
                dve.did(eng.tensor_copy(UU[0:R], b[0:R, 0:4]).then_inc(dve_done, 1), "drained", "uu", L, i)
                dve.wait_ge(pe_done, at("filled", "go", L, i))
                for c in range(2):
                    dve.wait_ge(pe_done, at("filled", "gs", L, i, c))
                    b = bank("gs", L, i, c)
                    tot = GSM[:, 132 + c * nb:132 + (c + 1) * nb]
                    if S:
                        dve.did(TT(GS[:, c], GS[:, c], bc(tot, 2, 64), ALU.mult).then_inc(dve_done, 1))
                        dve.wait_ge(dve_done, count("dve_done"))
                        dve.did(TT(GS[:, c], GS[:, c], b.rearrange("p (b v) -> p b v", b=NB), ALU.add).then_inc(dve_done, 1), "drained", "gs", L, i, c)
                    else:
                        dve.did(STT(GS[:, c, 0, :], GS[:, c, 0, :], tot, b[:, 0:64], ALU.mult, ALU.add).then_inc(dve_done, 1), "drained", "gs", L, i, c)
                if i < SAMPLE - 1:
                    counts.same(("gs_ready", L, i + 1), ("drained", "gs", L, i, 1))
                elif i == SAMPLE - 1:
                    counts.same(("gs_prompt", L), ("drained", "gs", L, i, 1))
                else:
                    counts.same(("gs_sample", L), ("drained", "gs", L, i, 1))
                dve.wait_ge(dve_done, count("dve_done"))
                head_out(L, i, "g", GRT, GON, GB, par("gnorm").broadcast_to([128, 2]), 2)

            for i in range(NT):
                for half in range(2):
                    add_h(L, i, half, "wo", 3 * L + 1)
            dve.wait_ge(sem("gs_s_stored"), at("gs2_out", L))
            norm(3 * L + 1)

            for i in range(NT):
                R = ROWS[i]
                s = SCO[0:R, i % 2, :].rearrange("p (h n) -> p h n", h=16)
                sv = SV[0:R, :].rearrange("p (h k) -> p h k", h=16)
                si = SI[0:R, :].rearrange("p (h k) -> p h k", h=16)
                for g in range(4):
                    dve.wait_ge(act_done, at("drained", "sc", L, i, g))
                for k0 in (0, 8):
                    for h in range(16):
                        dve.did(eng.max(out=sv[:, h, k0:k0 + 8], in_=s[:, h, :]).then_inc(dve_done, 1))
                    dve.wait_ge(dve_done, count("dve_done"))
                    for h in range(16):
                        dve.did(eng.max_index(out=si[:, h, k0:k0 + 8], in_max=sv[:, h, k0:k0 + 8], in_values=s[:, h, :]).then_inc(dve_done, 1))
                    dve.wait_ge(dve_done, count("dve_done"))
                    if k0 == 0:
                        for h in range(16):
                            dve.did(eng.match_replace(out=s[:, h, :], in_to_replace=sv[:, h, 0:8],
                                                      in_values=s[:, h, :], imm_value=-3.0e38).then_inc(dve_done, 1))
                        dve.wait_ge(dve_done, count("dve_done"))
                counts.marks[("topk", L, i)] = ("dve_done", count("dve_done"))
                dve.did(eng.tensor_copy(SIF[0:R, :], SI[0:R, :]).then_inc(dve_done, 1))
                sums = CAND[0:R, :].rearrange("p (h a b) -> p h a b", h=HEADS, a=TOPK)
                two = SV[0:R, :].rearrange("p (h q k) -> p h q k", h=HEADS, q=2)
                dve.did(TT(sums, bc(two[:, :, 0, :], 3, TOPK), bc(two[:, :, 1, :], 2, TOPK), ALU.add).then_inc(dve_done, 1))
                dve.wait_ge(dve_done, count("dve_done"))
                cand = CAND[0:R, :].rearrange("p (h n) -> p h n", h=HEADS)
                cv = CV[0:R, :].rearrange("p (h k) -> p h k", h=HEADS)
                ci = CI[0:R, :].rearrange("p (h k) -> p h k", h=HEADS)
                for k0 in (0, 8):
                    for h in range(HEADS):
                        dve.did(eng.max(out=cv[:, h, k0:k0 + 8], in_=cand[:, h, :]).then_inc(dve_done, 1))
                    dve.wait_ge(dve_done, count("dve_done"))
                    for h in range(HEADS):
                        dve.did(eng.max_index(out=ci[:, h, k0:k0 + 8], in_max=cv[:, h, k0:k0 + 8],
                                              in_values=cand[:, h, :]).then_inc(dve_done, 1))
                    dve.wait_ge(dve_done, count("dve_done"))
                    if k0 == 0:
                        for h in range(HEADS):
                            dve.did(eng.match_replace(out=cand[:, h, :], in_to_replace=cv[:, h, 0:8],
                                                      in_values=cand[:, h, :], imm_value=-3.0e38).then_inc(dve_done, 1))
                        dve.wait_ge(dve_done, count("dve_done"))
                dve.did(TS(CI2[0:R, 0, :], CI[0:R, :], 4, None, ALU.logical_shift_right).then_inc(dve_done, 1))
                dve.did(TS(CI2[0:R, 1, :], CI[0:R, :], 15, None, ALU.bitwise_and).then_inc(dve_done, 1))
                dve.wait_ge(dve_done, count("dve_done"))
                dve.did(eng.tensor_copy(CIF[0:R], CI2[0:R]).then_inc(dve_done, 1))
                if i:
                    dve.wait_ge(pe_done, at("filled", "it", L, i - 1))
                g3 = IGT[0:R, 2, :].rearrange("p (h k) -> p h k", h=HEADS)
                dve.did(TT(g3, cv, cv[:, :, 0:1].broadcast_to([R, HEADS, TOPK]), ALU.subtract).then_inc(dve_done, 1), "gsub", L, i)
                dve.wait_ge(dve_done, count("dve_done"))
                lists = SIF[0:R, :].rearrange("p (h q k) -> p h q k", h=HEADS, q=2)
                pick = PICK[0:R, :].rearrange("p (h k a) -> p h k a", h=HEADS, k=TOPK)
                flat = PICK[0:R, :].rearrange("p (n a) -> p n a", a=TOPK)
                for q in range(2):
                    place = CIF[0:R, q, :]
                    dve.did(TT(flat, bc(place, 2, TOPK), bc(const("iota")[0:R, 0:TOPK], 1, HEADS * TOPK), ALU.is_equal).then_inc(dve_done, 1))
                    dve.wait_ge(dve_done, count("dve_done"))
                    dve.did(TT(pick, pick, bc(lists[:, :, q, :], 2, TOPK), ALU.mult).then_inc(dve_done, 1))
                    dve.wait_ge(dve_done, count("dve_done"))
                    dve.did(eng.tensor_reduce(IGT[0:R, q, :], flat, AX, ALU.add).then_inc(dve_done, 1))
                    dve.wait_ge(dve_done, count("dve_done"))
                dve.wait_ge(act_done, at("gexp", L, i))
                dve.did(eng.tensor_reduce(GSUM[0:R, 0:8], g3, AX, ALU.add).then_inc(dve_done, 1))
                dve.wait_ge(dve_done, count("dve_done"))
                dve.did(eng.reciprocal(GSUM[0:R, 8:16], GSUM[0:R, 0:8]).then_inc(dve_done, 1))
                dve.wait_ge(dve_done, count("dve_done"))
                dve.did(TT(g3, g3, bc(GSUM[0:R, 8:16], 2, TOPK), ALU.mult).then_inc(dve_done, 1), "igt", L, i)
            counts.same(("topk_done", L), ("igt", L, NT - 1))
            for i in range(NT):
                dve.wait_ge(act_done, at("drained", "it", L, i))
            dve.wait_ge(pool_done, at("xr", L))
            with eng.Fori(0, NBLK) as b:
                nb_ = b + NBLK * L
                eng.wait_ge(oh2_ready, nb_ * 8 + 1)
                eng.wait_ge(oh1_ready, nb_ * 8 + 1)
                eng.tensor_copy(STG[:, :, :], IT[:, :, bass.ds(b * GBLK, GBLK)]).then_inc(staged, 1)
                eng.wait_ge(staged, nb_ + 1)
                for m in range(GBLK // 8):
                    eng.wait_ge(scattered, nb_ * 16 + (2 * m + 2))
                    for t in range(8):
                        ins = TS(OH1[:, m % 2, t, :], const("iota"), STG[:, 0, 8 * m + t:8 * m + t + 1],
                                 STG[:, 2, 8 * m + t:8 * m + t + 1], ALU.is_equal, ALU.mult)
                    ins.then_inc(oh1_ready, 1)
            eng.wait_ge(scattered, 16 * NBLK * (L + 1) + 4)
            for j in range(3):
                eng.wait_ge(d_gstore[j], 16 * (NBLK // 3 * (L + 1) + 1))
            dve.did(eng.memset(ACC[:, :, :], 0.0).then_inc(dve_done, 1))
            dve.wait_ge(dve_done, count("dve_done"))
            counts.marks[("hm_free", L)] = ("dve_done", count("dve_done"))

            def gate_row(g, par_, i, gate_base):
                row = (g + NGROUPS * L) * GROUP + i
                eng.wait_ge(gelu_done, row + 3)
                if i == 0:
                    eng.wait_ge(d_gload[par_], gate_base)
                gt = GT[:, par_].rearrange("p b (i t) -> p b i t", i=GROUP)[:, :, i, :]
                ge = GE[:, i % 2, :].rearrange("p (b t) -> p b t", b=NBLK)
                TT(ge, ge, gt, ALU.mult).then_inc(gated, 1)
                eng.wait_ge(v_done, (g + NGROUPS * L) * KT + KT)
                eng.wait_ge(gated, row + 1)
                eng.tensor_copy(HR[:, par_ * GROUP + i, 0, :], GE[:, i % 2, :]).then_inc(gated_rounded, 1)
                eng.wait_ge(gated_rounded, row + 1)
                TT(HR[:, par_ * GROUP + i, 1, :], GE[:, i % 2, :], HR[:, par_ * GROUP + i, 0, :].bitcast(F32),
                   ALU.subtract).then_inc(hm_done, 1)

            def add_tile(g, dt_):
                n = (g + NGROUPS * L) * KT + dt_
                eng.wait_ge(v_done, n + (1 + 2 * KT))
                acc = ACC[:, dt_, :].rearrange("p (c t) -> p c t", c=2)
                TT(acc, acc, PS[:, 4 + 2 * (dt_ % 2):6 + 2 * (dt_ % 2), 0:HALF], ALU.add).then_inc(acc_done, 1)

            for i in range(GROUP):
                gate_row(0, 0, i, 16 * (1 + NGROUPS // 2 * L))
            with eng.Fori(0, NGROUPS // 2 - 1) as it:
                for par_ in range(2):
                    g = it * 2 + par_
                    for i in range(GROUP):
                        add_tile(g, TPR * i)
                        add_tile(g, TPR * i + 1)
                        gate_row(g + 1, 1 - par_, i, (it + (par_ + NGROUPS // 2 * L)) * 16 + 16)
                        add_tile(g, TPR * i + 2)
                        add_tile(g, TPR * i + 3)
            for g in (NGROUPS - 2, NGROUPS - 1):
                for i in range(GROUP):
                    for dt_ in range(TPR * i, TPR * (i + 1)):
                        add_tile(g, dt_)
                        if g == NGROUPS - 2 and dt_ == TPR * i + 1:
                            gate_row(g + 1, 1, i, 16 * (NGROUPS // 2) * (L + 1))
            eng.wait_ge(acc_done, KT * NGROUPS * (L + 1) + 2)
            for i in range(NT):
                for half in range(2):
                    add_h(L, i, half, "back", 3 * L + 2)
            norm(3 * L + 2)
            for i in range(NT):
                R = ROWS[i]
                for half in range(2):
                    hs = slice(half * 512, (half + 1) * 512)
                    dve.wait_ge(pe_done, at("filled", "pp", L, i, half))
                    b = bank("pp", L, i, half)
                    dve.wait_ge(act_done, at("drained", "pg", L, i, half))
                    dve.did(TT(TP[0:R, i % 2, hs], SG[0:R, i % 2, hs], b[0:R, :], ALU.mult).then_inc(dve_done, 1), "drained", "pp", L, i, half)
                    dve.wait_ge(dve_done, count("dve_done"))
                    dve.did(TT(H[0:R, i, hs], H[0:R, i, hs], TP[0:R, i % 2, hs], ALU.add).then_inc(dve_done, 1), *(("h", 3 * L + 3, i) if half else ()))
            counts.same(("ple_done", L), ("h", 3 * L + 3, NT - 1))
        dve.wait_ge(sem("gf_loaded"), at("gf"))
        for i in range(NT):
            R = ROWS[i]
            dve.wait_ge(act_done, at("rms", 3 * DEPTH, i))
            dve.did(eng.reciprocal(SS[0:R, 10 + i:11 + i], SS[0:R, 5 + i:6 + i]).then_inc(dve_done, 1))
            dve.wait_ge(dve_done, count("dve_done"))
            dve.did(STT(XN[0:R, i % 2, :], H[0:R, i, :], SS[0:R, 10 + i:11 + i], GF[0:R, :], ALU.mult, ALU.mult).then_inc(dve_done, 1), "y", i)

    ctx.close()
    return {"marks": counts.marks, "banks": {label: n % 8 for n, label in enumerate(fills["order"])}}


def inputs_laid_out(x):
    f = np.ascontiguousarray
    a = {}
    a["x_prompt"] = x["x_prompt"].reshape(SEQ, D)
    a["x_sample"] = x["x_sample"].reshape(SAM, D)
    a["consts"] = constants()[1]
    w = x["w_in"]
    o = np.cumsum([0, 256, 256, 256, 256, 768, 256, 4, 4, 512, 256])
    start = {"q": o[0], "f": o[1], "i": o[2], "ga": o[3], "k": o[4], "gb": o[5], "bb": o[6], "ba": o[7],
             "ca": o[8], "cb": o[8] + 256, "p": o[9]}
    tiles = []
    for name in FM:
        c0 = start[name[:-1]] + 128 * int(name[-1])
        tiles.append(w[:, :, c0:c0 + 128].reshape(DEPTH, KT, 128, 128).transpose(0, 2, 1, 3).reshape(DEPTH, 128, D))
    a["w_fm"] = f(np.stack(tiles, 1))
    tm = np.concatenate([w[:, :, o[2]:o[2] + 256], w[:, :, o[6]:o[6] + 8]], 2)
    kt = lambda m: f(m.reshape(DEPTH, m.shape[1] // 128, 128, m.shape[2]).transpose(0, 2, 1, 3))
    a["w_tm"] = kt(tm)
    a["w_out"] = kt(x["w_out"])
    a["ple_gate"] = kt(x["ple_gate_w"])
    a["ple_proj"] = kt(x["ple_proj_w"])
    a["peer_wq"] = f(x["peer_wq"].reshape(DEPTH, KT, 128, HEADS, 128).transpose(0, 3, 2, 1, 4)
                     .reshape(DEPTH, HEADS, 128, D))
    a["peer_keys"] = f(x["peer_keys"].transpose(0, 2, 4, 1, 3).reshape(DEPTH, 128, HEADS, NKEYS))
    a["peer_ut"] = f(x["peer_u"].reshape(DEPTH, NKEYS, NKEYS, KT, 128).transpose(0, 1, 4, 3, 2)
                     .reshape(DEPTH, NKEYS, 128, D))
    a["peer_v"] = x["peer_v"].reshape(DEPTH, NKEYS, NKEYS, D)
    p = np.concatenate([x["p_prompt"].reshape(DEPTH, SEQ, 256), x["p_sample"].reshape(DEPTH, SAM, 256)], 1)
    a["p_t"] = f(p.reshape(DEPTH, TOK, 2, 128).transpose(0, 3, 2, 1))
    state = lambda s: f(s.reshape(DEPTH, NB, 2, 2, 64, 64).transpose(0, 3, 4, 2, 1, 5).reshape(DEPTH, 128, 2, NB, 64))
    a["s_hgrn"], a["s_gdn"] = state(x["state_hgrn"]), state(x["state_gdn"])
    rows = lambda s: f(s.reshape(DEPTH, NB, s.shape[2], -1, 128).transpose(0, 4, 3, 1, 2))
    a["s_qkv"], a["s_conf"], a["s_pool"] = (rows(x[k]) for k in ("state_gdn_conv", "state_conf_conv", "state_pool"))
    col = lambda v: v.reshape(DEPTH, -1, 128).transpose(0, 2, 1)
    taps = lambda v: v.reshape(DEPTH, v.shape[1], -1, 128).transpose(0, 3, 2, 1).reshape(DEPTH, 128, -1)
    every = lambda v: np.broadcast_to(v[:, None, :], (DEPTH, 128, v.shape[-1]))
    logits = np.broadcast_to(x["hgrn_lb_logits"].reshape(DEPTH, 2, 128).transpose(2, 0, 1).reshape(1, 128, 4),
                             (DEPTH, 128, 4))
    poolw = x["pool_w"].reshape(DEPTH, 2, 2, 64, 64).transpose(0, 2, 3, 1, 4).reshape(DEPTH, 128, 128)
    a["params"] = f(np.concatenate(
        [col(x["norm_mix"]), col(x["norm_ffn"]), col(x["norm_ple"]), col(x["hgrn_norm"]),
         np.concatenate([x["gdn_norm"], x["gdn_norm"]], 1)[:, :, None], taps(x["gdn_conv_w"]), taps(x["conf_dw_w"]),
         col(x["conf_dw_b"]), col(x["conf_ln_g"]), col(x["conf_ln_b"]), col(x["pool_scale"]), poolw,
         every(x["gdn_a_log"]), every(x["gdn_dt_bias"]), logits], 2))
    a["norm_final"] = f(np.broadcast_to(x["norm_final"][None, :], (128, D)))
    return a


OUTPUTS = {"y_prompt": (SEQ, D), "y_sample": (SAM, D), "hgrn_p": (DEPTH, 128, 2, 64), "gdn_p": (DEPTH, 128, 2, 64),
           "qkv_p": (DEPTH, 128, 6, BCONV - 1), "conf_p": (DEPTH, 128, 2, CCONV - 1), "pool_p": (DEPTH, 128, 2, POOLB),
           "hgrn_s": (DEPTH, 128, 2, NB, 64), "gdn_s": (DEPTH, 128, 2, NB, 64),
           "qkv_s": (DEPTH, 128, 6, NB, BCONV - 1), "conf_s": (DEPTH, 128, 2, NB, CCONV - 1),
           "pool_s": (DEPTH, 128, 2, NB, POOLB)}


def declared(nc, shapes):
    din = {k: nc.dram_tensor(k, v, F32, kind="ExternalInput").ap() for k, v in shapes.items()}
    dout = {k: nc.dram_tensor(k, v, F32, kind="ExternalOutput").ap() for k, v in OUTPUTS.items()}
    gates = nc.dram_tensor("gates", (NBLK, NKEYS, NKEYS, GBLK), F32, kind="Internal").ap()
    return din, dout, gates


def kernel(**inputs):
    import concourse.bacc as bacc
    from concourse.bass_utils import run_bass_kernel_spmd

    arrays = inputs_laid_out({k: np.asarray(v) for k, v in inputs.items()})
    shapes = {k: v.shape for k, v in arrays.items()}
    scratch = bacc.Bacc("TRN2", target_bir_lowering=False, num_devices=1)
    known = trunk(scratch, *declared(scratch, shapes), None)
    nc = bacc.Bacc("TRN2", target_bir_lowering=False, num_devices=1)
    trunk(nc, *declared(nc, shapes), known)
    r = run_bass_kernel_spmd(nc, [arrays], core_ids=[0]).results[0]
    sp = lambda s: s.reshape(DEPTH, 2, 64, 2, 1, 64).transpose(0, 4, 3, 1, 2, 5).reshape(DEPTH, 1, 4, 64, 64)
    ss = lambda s: s.reshape(DEPTH, 2, 64, 2, NB, 64).transpose(0, 4, 3, 1, 2, 5).reshape(DEPTH, NB, 4, 64, 64)
    bp = lambda s: s.transpose(0, 3, 2, 1).reshape(DEPTH, 1, s.shape[3], -1)
    bs = lambda s: s.transpose(0, 3, 4, 2, 1).reshape(DEPTH, NB, s.shape[4], -1)
    return (r["y_prompt"].reshape(1, SEQ, D), r["y_sample"].reshape(NB, NS, D),
            sp(r["hgrn_p"]), sp(r["gdn_p"]), bp(r["qkv_p"]), bp(r["conf_p"]), bp(r["pool_p"]),
            ss(r["hgrn_s"]), ss(r["gdn_s"]), bs(r["qkv_s"]), bs(r["conf_s"]), bs(r["pool_s"]))
```
